# Optimizing a Trainium2 kernel written in Bass

```python
import jax, jax.numpy as jnp
from jax import lax
import numpy as np
import math

D_MODEL = 1024
BATCH = 1
SEQ = 256
DEPTH = 2

CHUNK = 64
SUB_CHUNK = 16
POOL_WIDTH = 512
POOL_GROUPS = 4
POOL_WINDOWS = (2, 4, 8, 16)
POOL_GROUP_DIM = POOL_WIDTH // POOL_GROUPS
HGRN_HEADS = 4
HGRN_EXPAND = 128
HGRN_HEAD_DIM = 128
HGRN_FORGET = HGRN_HEADS * HGRN_EXPAND
HGRN_INPUT = HGRN_HEADS * HGRN_HEAD_DIM
N_BRANCHES = 2
D_IN = POOL_WIDTH + 2 * HGRN_FORGET + 2 * HGRN_INPUT + N_BRANCHES * D_MODEL
D_FF = 2816
EPS = 1e-6


def rmsnorm(x, g):
    xf = x.astype(jnp.float32)
    y = xf * lax.rsqrt(jnp.mean(xf * xf, axis=-1, keepdims=True) + EPS)
    return (y * g.astype(jnp.float32)).astype(x.dtype)

def swiglu(x, w_gate, w_up, w_down):
    return (jax.nn.silu(x @ w_gate) * (x @ w_up)) @ w_down

def causal_pool_mixer(u, pool_w, pool_scale):
    b_, s_, _ = u.shape
    ug = u.reshape(b_, s_, POOL_GROUPS, POOL_GROUP_DIM)
    cs = jnp.cumsum(ug.astype(jnp.float32), axis=1)
    cs = jnp.pad(cs, ((0, 0), (1, 0), (0, 0), (0, 0)))
    pos = jnp.arange(1, s_ + 1)
    means = []
    for g, w in enumerate(POOL_WINDOWS):
        lo = jnp.maximum(pos - w, 0)
        window_sum = cs[:, 1:, g] - cs[:, lo, g]
        count = (pos - lo).astype(jnp.float32)
        means.append(window_sum / count[None, :, None])
    pooled = jnp.stack(means, axis=2).astype(u.dtype)
    mixed = jnp.einsum('bsgc,gcd->bsgd', pooled - ug, pool_w)
    return mixed.reshape(b_, s_, POOL_WIDTH) * pool_scale

def hgrn2_chunkwise(q, k, v, log_f):
    b_, h_, s_, dk = q.shape
    dv = v.shape[-1]
    n = s_ // CHUNK
    ns = CHUNK // SUB_CHUNK
    qc = q.reshape(b_, h_, n, CHUNK, dk)
    kc = k.reshape(b_, h_, n, CHUNK, dk)
    vc = v.reshape(b_, h_, n, CHUNK, dv)
    b = jnp.cumsum(log_f.reshape(b_, h_, n, CHUNK, dk), axis=3)
    b_last = b[:, :, :, -1]

    k_to_end = kc * jnp.exp(b_last[:, :, :, None] - b)
    u_chunk = jnp.einsum('bhnck,bhncv->bhnkv', k_to_end, vc)
    decay = jnp.exp(b_last)

    def step(state, inp):
        d, u = inp
        return d[..., None] * state + u, state

    s0 = jnp.zeros((b_, h_, dk, dv), q.dtype)
    _, s_prev = lax.scan(step, s0, (jnp.moveaxis(decay, 2, 0), jnp.moveaxis(u_chunk, 2, 0)))
    s_prev = jnp.moveaxis(s_prev, 0, 2)
    o_state = jnp.einsum('bhnck,bhnkv->bhncv', qc * jnp.exp(b), s_prev)

    bs = b.reshape(b_, h_, n, ns, SUB_CHUNK, dk)
    qs = qc.reshape(b_, h_, n, ns, SUB_CHUNK, dk)
    ks = kc.reshape(b_, h_, n, ns, SUB_CHUNK, dk)
    vs = vc.reshape(b_, h_, n, ns, SUB_CHUNK, dv)
    b_ref = jnp.concatenate([jnp.zeros_like(bs[:, :, :, :1, -1]), bs[:, :, :, :-1, -1]], axis=3)
    q_ref = qs * jnp.exp(bs - b_ref[..., None, :])
    sub_id = jnp.arange(CHUNK) // SUB_CHUNK
    earlier = sub_id[None, :] < jnp.arange(ns)[:, None]
    k_exp = jnp.where(earlier[:, :, None],
                      b_ref[:, :, :, :, None, :] - b[:, :, :, None, :, :], -jnp.inf)
    k_ref = kc[:, :, :, None] * jnp.exp(k_exp)
    a_cross = jnp.einsum('bhnitk,bhnisk->bhnits', q_ref, k_ref)
    o_cross = jnp.einsum('bhnits,bhnsv->bhnitv', a_cross, vc)

    tril = jnp.tril(jnp.ones((SUB_CHUNK, SUB_CHUNK), bool))
    rel = jnp.where(tril[:, :, None], bs[..., :, None, :] - bs[..., None, :, :], -jnp.inf)
    a_diag = jnp.sum(qs[..., :, None, :] * ks[..., None, :, :] * jnp.exp(rel), axis=-1)
    o_diag = jnp.einsum('bhnits,bhnisv->bhnitv', a_diag, vs)

    o = o_state + (o_cross + o_diag).reshape(b_, h_, n, CHUNK, dv)
    return o.reshape(b_, h_, s_, dv)

def hybrid_mixer(h, w_in, pool_w, pool_scale, lb, hgrn_norm, w_pool_proj, w_hgrn_proj, w_out):
    b_, s_, _ = h.shape
    z = h @ w_in
    splits = [POOL_WIDTH, POOL_WIDTH + HGRN_FORGET, POOL_WIDTH + 2 * HGRN_FORGET,
              POOL_WIDTH + 2 * HGRN_FORGET + HGRN_INPUT, POOL_WIDTH + 2 * HGRN_FORGET + 2 * HGRN_INPUT]
    u_pool, q_pre, f_pre, i_in, og, gates = jnp.split(z, splits, axis=-1)

    pool_out = causal_pool_mixer(u_pool, pool_w, pool_scale)

    def heads(t, d):
        return t.reshape(b_, s_, HGRN_HEADS, d).transpose(0, 2, 1, 3).astype(jnp.float32)

    fz = heads(f_pre, HGRN_EXPAND)
    lbh = lb.astype(jnp.float32).reshape(HGRN_HEADS, 1, HGRN_EXPAND)
    log_f = jnp.logaddexp(jnp.log(lbh), jnp.log1p(-lbh) + jax.nn.log_sigmoid(fz))
    k = (1.0 - lbh) * jax.nn.sigmoid(-fz)
    q = jax.nn.silu(heads(q_pre, HGRN_EXPAND))
    v = heads(i_in, HGRN_HEAD_DIM)
    o = hgrn2_chunkwise(q, k, v, log_f)
    o = o * lax.rsqrt(jnp.mean(o * o, axis=-1, keepdims=True) + EPS)
    o = o.transpose(0, 2, 1, 3).reshape(b_, s_, HGRN_INPUT) * hgrn_norm.astype(jnp.float32)
    hgrn_out = (o * jax.nn.silu(og.astype(jnp.float32))).astype(h.dtype)

    g = jax.nn.sigmoid(gates).reshape(b_, s_, N_BRANCHES, D_MODEL)
    merged = g[:, :, 0] * (pool_out @ w_pool_proj) + g[:, :, 1] * (hgrn_out @ w_hgrn_proj)
    return merged @ w_out

def first_inputs(seed: int = 0) -> dict:
    key = jax.random.key(seed)
    ks = jax.random.split(key, 20)

    def nrm(k, shape, fan_in):
        return jax.random.normal(k, shape, jnp.float32) * fan_in ** -0.5

    def gain(k, shape):
        return 1.0 + 0.05 * jax.random.normal(k, shape, jnp.float32)

    L, D = DEPTH, D_MODEL
    return {
        'x': jax.random.normal(ks[0], (BATCH, SEQ, D), jnp.float32),
        'ffn1_norm': gain(ks[1], (L, D)),
        'ffn1_w_gate': nrm(ks[2], (L, D, D_FF), D),
        'ffn1_w_up': nrm(ks[3], (L, D, D_FF), D),
        'ffn1_w_down': nrm(ks[4], (L, D_FF, D), D_FF),
        'mix_norm': gain(ks[5], (L, D)),
        'w_in': nrm(ks[6], (L, D, D_IN), D),
        'pool_w': nrm(ks[7], (L, POOL_GROUPS, POOL_GROUP_DIM, POOL_GROUP_DIM), POOL_GROUP_DIM),
        'pool_scale': gain(ks[8], (L, POOL_WIDTH)),
        'lb_logits': 0.5 * jax.random.normal(ks[9], (L, HGRN_FORGET), jnp.float32),
        'hgrn_norm': gain(ks[10], (L, HGRN_INPUT)),
        'w_pool_proj': nrm(ks[11], (L, POOL_WIDTH, D), POOL_WIDTH),
        'w_hgrn_proj': nrm(ks[12], (L, HGRN_INPUT, D), HGRN_INPUT),
        'w_out': nrm(ks[13], (L, D, D), D),
        'ffn2_norm': gain(ks[14], (L, D)),
        'ffn2_w_gate': nrm(ks[15], (L, D, D_FF), D),
        'ffn2_w_up': nrm(ks[16], (L, D, D_FF), D),
        'ffn2_w_down': nrm(ks[17], (L, D_FF, D), D_FF),
        'final_norm': gain(ks[18], (D,)),
    }

def first_block(x, ffn1_norm, ffn1_w_gate, ffn1_w_up, ffn1_w_down, mix_norm, w_in, pool_w,
              pool_scale, lb_logits, hgrn_norm, w_pool_proj, w_hgrn_proj, w_out,
              ffn2_norm, ffn2_w_gate, ffn2_w_up, ffn2_w_down, final_norm):
    lb_all = jnp.cumsum(jax.nn.softmax(lb_logits.astype(jnp.float32), axis=0), axis=0)
    lb_all = lb_all - lb_all[:1]
    for l in range(DEPTH):
        x = x + 0.5 * swiglu(rmsnorm(x, ffn1_norm[l]), ffn1_w_gate[l], ffn1_w_up[l], ffn1_w_down[l])
        h = rmsnorm(x, mix_norm[l])
        x = x + hybrid_mixer(h, w_in[l], pool_w[l], pool_scale[l], lb_all[l], hgrn_norm[l],
                             w_pool_proj[l], w_hgrn_proj[l], w_out[l])
        x = x + 0.5 * swiglu(rmsnorm(x, ffn2_norm[l]), ffn2_w_gate[l], ffn2_w_up[l], ffn2_w_down[l])
    return rmsnorm(x, final_norm)


MEM_LEN = 256
BLOCK_Q = 128
H_A = 8
DH_A = 64
DC_A = 128
H_IDX = 8
DH_IDX = 64
TOPK_MAX = 256
H_SB = 8
DH_SB = 64
C_CONV = 512
CONV_W = 3
W_A = H_A * DH_A
W_SB = H_SB * DH_SB
W_BRANCH = 512
N_BRANCH = 3
H_X = 4
DH_X = 128
N_BUCKETS = 32
MAX_DISTANCE = 128
DN_ALPHA = (2 * DEPTH) ** 0.25
DN_BETA = (8 * DEPTH) ** -0.25
LN_EPS = 1e-5
N_LN = 4
SPLITS = (W_A, DC_A, H_IDX * DH_IDX, DH_IDX, H_IDX, W_SB, W_SB, W_SB,
          C_CONV, C_CONV, C_CONV, D_MODEL, D_MODEL, D_MODEL)
P_TOTAL = sum(SPLITS)


def layer_norm(x, g, b):
    xf = x.astype(jnp.float32)
    mu = jnp.mean(xf, axis=-1, keepdims=True)
    var = jnp.mean(jnp.square(xf - mu), axis=-1, keepdims=True)
    y = (xf - mu) * lax.rsqrt(var + LN_EPS) * g.astype(jnp.float32) + b.astype(jnp.float32)
    return y.astype(x.dtype)

def rms_norm(x, g):
    xf = x.astype(jnp.float32)
    y = xf * lax.rsqrt(jnp.mean(jnp.square(xf), axis=-1, keepdims=True) + LN_EPS) * g.astype(jnp.float32)
    return y.astype(x.dtype)

def swiglu_ffn(x, w_in, w_out):
    a, b = jnp.split(x @ w_in, 2, axis=-1)
    return (jax.nn.silu(a) * b) @ w_out

def t5_bucket(n):
    max_exact = N_BUCKETS // 2
    n = jnp.maximum(n, 0)
    nf = jnp.maximum(n, 1).astype(jnp.float32)
    large = max_exact + (jnp.log(nf / max_exact) / math.log(MAX_DISTANCE / max_exact)
                         * (N_BUCKETS - max_exact)).astype(jnp.int32)
    large = jnp.minimum(large, N_BUCKETS - 1)
    return jnp.where(n < max_exact, n, large)

def dsa_branch(q, c_kv, iq, ik, iw, w_uk, w_uv, rel_bias):
    bsz, seq = q.shape[0], q.shape[1]
    k_top = min(TOPK_MAX, seq // 4)
    nblk = seq // BLOCK_Q
    q_lat = jnp.einsum('bshd,hdc->bshc', q, w_uk) * (DH_A ** -0.5)
    idx_scale = (H_IDX ** -0.5) * (DH_IDX ** -0.5)

    def to_blocks(a):
        return jnp.swapaxes(a.reshape((bsz, nblk, BLOCK_Q) + a.shape[2:]), 0, 1)

    starts = jnp.arange(nblk, dtype=jnp.int32) * BLOCK_Q
    key_pos = jnp.arange(seq, dtype=jnp.int32)

    def block(args):
        ql, iqb, iwb, start = args
        t = start + jnp.arange(BLOCK_Q, dtype=jnp.int32)
        causal = key_pos[None, :] <= t[:, None]
        dots = jnp.einsum('bqhd,bsd->bhqs', iqb, ik).astype(jnp.float32)
        score = jnp.einsum('bqh,bhqs->bqs', iwb.astype(jnp.float32) * idx_scale, jax.nn.relu(dots))
        score = jnp.where(causal[None], score, -jnp.inf)
        _, idx = lax.top_k(score, k_top)
        valid = idx <= t[None, :, None]
        kv_sel = jax.vmap(lambda c, i: c[i])(c_kv, idx)
        logits = jnp.einsum('bqhc,bqkc->bhqk', ql, kv_sel).astype(jnp.float32)
        bias = rel_bias[t5_bucket(t[None, :, None] - idx)]
        logits = logits + jnp.transpose(bias, (0, 3, 1, 2)).astype(jnp.float32)
        logits = jnp.where(valid[:, None], logits, -1e30)
        p = jax.nn.softmax(logits, axis=-1).astype(kv_sel.dtype)
        return jnp.einsum('bhqk,bqkc->bqhc', p, kv_sel)

    o_lat = lax.map(block, (to_blocks(q_lat), to_blocks(iq), to_blocks(iw), starts))
    o_lat = jnp.swapaxes(o_lat, 0, 1).reshape(bsz, seq, H_A, DC_A)
    o = jnp.einsum('bshc,hcd->bshd', o_lat, w_uv)
    return o.reshape(bsz, seq, W_A)

def stick_breaking_branch(q, k, v):
    bsz, seq = q.shape[0], q.shape[1]
    scale = DH_SB ** -0.5
    outs = []
    for i in range(seq // BLOCK_Q):
        q0 = i * BLOCK_Q
        end = q0 + BLOCK_Q
        z = jnp.einsum('bqhd,bshd->bhqs', q[:, q0:end], k[:, :end]).astype(jnp.float32) * scale
        t = q0 + jnp.arange(BLOCK_Q)
        s = jnp.arange(end)
        strict = (s[None, :] < t[:, None])[None, None]
        log_not = jnp.where(strict, jax.nn.log_sigmoid(-z), 0.0)
        later = lax.cumsum(log_not, axis=3, reverse=True) - log_not
        a = jnp.where(strict, jnp.exp(jax.nn.log_sigmoid(z) + later), 0.0)
        outs.append(jnp.einsum('bhqs,bshd->bqhd', a.astype(v.dtype), v[:, :end]))
    return jnp.concatenate(outs, axis=1).reshape(bsz, seq, W_SB)

def short_conv_branch(b_gate_in, c_gate_in, h, conv_w):
    z = c_gate_in * h
    y = lax.conv_general_dilated(z, conv_w[:, None, :].astype(z.dtype), window_strides=(1,),
                                 padding=((CONV_W - 1, 0),),
                                 dimension_numbers=('NWC', 'WIO', 'NWC'),
                                 feature_group_count=C_CONV)
    return b_gate_in * y

def mixer_sublayer(x, w_in, b_gate, kv_g, w_uk, w_uv, conv_w, w_branch, w_out, rel_bias):
    bsz, seq = x.shape[0], x.shape[1]
    offsets = [int(o) for o in np.cumsum(SPLITS)[:-1]]
    (qa, ckv, iq, ik, iw, qs, ks, vs, cb, cc, ch, ga, gb, gc) = jnp.split(x @ w_in, offsets, axis=-1)
    ckv = rms_norm(ckv, kv_g)
    y_a = dsa_branch(qa.reshape(bsz, seq, H_A, DH_A), ckv,
                     iq.reshape(bsz, seq, H_IDX, DH_IDX), ik, iw, w_uk, w_uv, rel_bias)
    hs = (bsz, seq, H_SB, DH_SB)
    y_b = stick_breaking_branch(qs.reshape(hs), ks.reshape(hs), vs.reshape(hs))
    y_c = short_conv_branch(cb, cc, ch, conv_w)
    merged = (jax.nn.sigmoid(ga + b_gate[0]) * (y_a @ w_branch[0])
              + jax.nn.sigmoid(gb + b_gate[1]) * (y_b @ w_branch[1])
              + jax.nn.sigmoid(gc + b_gate[2]) * (y_c @ w_branch[2]))
    return merged @ w_out

def memory_cross_attention(x, mem, wq, wkv, wo):
    bsz, seq = x.shape[0], x.shape[1]
    q = (x @ wq).reshape(bsz, seq, H_X, DH_X)
    k, v = jnp.split(mem @ wkv, 2, axis=-1)
    k = k.reshape(bsz, mem.shape[1], H_X, DH_X)
    v = v.reshape(bsz, mem.shape[1], H_X, DH_X)
    logits = jnp.einsum('bqhd,bmhd->bhqm', q, k).astype(jnp.float32) * (DH_X ** -0.5)
    p = jax.nn.softmax(logits, axis=-1).astype(v.dtype)
    o = jnp.einsum('bhqm,bmhd->bqhd', p, v).reshape(bsz, seq, H_X * DH_X)
    return o @ wo

def second_inputs(seed: int = 0) -> dict:
    key = jax.random.key(seed)
    ks = jax.random.split(key, 20)
    n = jax.random.normal
    f32 = jnp.float32
    return {
        "x": n(ks[0], (BATCH, SEQ, D_MODEL), f32),
        "mem": n(ks[1], (BATCH, MEM_LEN, D_MODEL), f32),
        "ln_g": 1.0 + 0.01 * n(ks[2], (DEPTH, N_LN, D_MODEL), f32),
        "ln_b": 0.01 * n(ks[3], (DEPTH, N_LN, D_MODEL), f32),
        "ffn_w_in": n(ks[4], (DEPTH, 2, D_MODEL, 2 * D_FF), f32) * D_MODEL ** -0.5,
        "ffn_w_out": n(ks[5], (DEPTH, 2, D_FF, D_MODEL), f32) * (D_FF ** -0.5 * DN_BETA),
        "w_mix_in": n(ks[6], (DEPTH, D_MODEL, P_TOTAL), f32) * D_MODEL ** -0.5,
        "b_gate": 0.01 * n(ks[7], (DEPTH, N_BRANCH, D_MODEL), f32),
        "kv_norm_g": 1.0 + 0.01 * n(ks[8], (DEPTH, DC_A), f32),
        "w_uk": n(ks[9], (DEPTH, H_A, DH_A, DC_A), f32) * DH_A ** -0.5,
        "w_uv": n(ks[10], (DEPTH, H_A, DC_A, DH_A), f32) * DC_A ** -0.5,
        "conv_w": n(ks[11], (DEPTH, CONV_W, C_CONV), f32) * CONV_W ** -0.5,
        "w_branch": n(ks[12], (DEPTH, N_BRANCH, W_BRANCH, D_MODEL), f32) * W_BRANCH ** -0.5,
        "w_mix_out": n(ks[13], (DEPTH, D_MODEL, D_MODEL), f32) * (D_MODEL ** -0.5 * DN_BETA),
        "xa_wq": n(ks[14], (DEPTH, D_MODEL, H_X * DH_X), f32) * D_MODEL ** -0.5,
        "xa_wkv": n(ks[15], (DEPTH, D_MODEL, 2 * H_X * DH_X), f32) * D_MODEL ** -0.5,
        "xa_wo": n(ks[16], (DEPTH, H_X * DH_X, D_MODEL), f32) * ((H_X * DH_X) ** -0.5 * DN_BETA),
        "rel_bias": 0.1 * n(ks[17], (N_BUCKETS, H_A), f32),
    }

def second_block(x, mem, ln_g, ln_b, ffn_w_in, ffn_w_out, w_mix_in, b_gate, kv_norm_g, w_uk, w_uv,
              conv_w, w_branch, w_mix_out, xa_wq, xa_wkv, xa_wo, rel_bias):
    for l in range(DEPTH):
        x = layer_norm(DN_ALPHA * x + 0.5 * swiglu_ffn(x, ffn_w_in[l, 0], ffn_w_out[l, 0]),
                       ln_g[l, 0], ln_b[l, 0])
        x = layer_norm(DN_ALPHA * x + mixer_sublayer(x, w_mix_in[l], b_gate[l], kv_norm_g[l], w_uk[l],
                                                     w_uv[l], conv_w[l], w_branch[l], w_mix_out[l],
                                                     rel_bias),
                       ln_g[l, 1], ln_b[l, 1])
        x = layer_norm(DN_ALPHA * x + memory_cross_attention(x, mem, xa_wq[l], xa_wkv[l], xa_wo[l]),
                       ln_g[l, 2], ln_b[l, 2])
        x = layer_norm(DN_ALPHA * x + 0.5 * swiglu_ffn(x, ffn_w_in[l, 1], ffn_w_out[l, 1]),
                       ln_g[l, 3], ln_b[l, 3])
    return x


def setup_inputs(seed=0):
    out = dict(first_inputs(seed))
    for name, value in second_inputs(seed + 1).items():
        if name != "x":
            out[name + "_2"] = value
    return out


def reference(
    x, ffn1_norm, ffn1_w_gate, ffn1_w_up, ffn1_w_down, mix_norm, w_in, pool_w, pool_scale,
    lb_logits, hgrn_norm, w_pool_proj, w_hgrn_proj, w_out, ffn2_norm, ffn2_w_gate, ffn2_w_up,
    ffn2_w_down, final_norm, mem_2, ln_g_2, ln_b_2, ffn_w_in_2, ffn_w_out_2, w_mix_in_2,
    b_gate_2, kv_norm_g_2, w_uk_2, w_uv_2, conv_w_2, w_branch_2, w_mix_out_2, xa_wq_2, xa_wkv_2,
    xa_wo_2, rel_bias_2,
):
    x = first_block(
        x, ffn1_norm, ffn1_w_gate, ffn1_w_up, ffn1_w_down, mix_norm, w_in, pool_w, pool_scale,
        lb_logits, hgrn_norm, w_pool_proj, w_hgrn_proj, w_out, ffn2_norm, ffn2_w_gate,
        ffn2_w_up, ffn2_w_down, final_norm,
    )
    return second_block(
        x, mem_2, ln_g_2, ln_b_2, ffn_w_in_2, ffn_w_out_2, w_mix_in_2, b_gate_2, kv_norm_g_2,
        w_uk_2, w_uv_2, conv_w_2, w_branch_2, w_mix_out_2, xa_wq_2, xa_wkv_2, xa_wo_2,
        rel_bias_2,
    )


_drawn_inputs = setup_inputs


def setup_inputs(seed=0):
    import zlib

    import numpy as np

    out = dict(_drawn_inputs(seed))
    spreads = {}
    factors = {'lb_logits': 3.286, 'b_gate_2': 8.0, 'kv_norm_g_2': 8.0, 'rel_bias_2': 8.0}
    for name, (base, spread) in spreads.items():
        noise = np.random.default_rng([zlib.crc32(name.encode()), seed]).standard_normal(out[name].shape)
        drawn = base * np.exp(spread * noise) if base else spread * noise
        out[name] = __import__('jax').numpy.asarray(drawn.astype(out[name].dtype))
    for name, factor in factors.items():
        out[name] = (out[name] * factor).astype(out[name].dtype)
    return out
```

```python
import numpy as np
from contextlib import ExitStack

import concourse.bass as bass
from concourse import mybir

F32 = mybir.dt.float32
F32R = mybir.dt.float32r
U32 = mybir.dt.uint32
ACT = mybir.ActivationFunctionType
ALU = mybir.AluOpType
AXX = mybir.AxisListType.X

P = 128
S = 256
D = 1024
KD = D // P
DFF = 2816
KF = DFF // P
LAYERS = 2
HW = 512
HEADS1 = 4
EPS1 = 1e-6
EPS2 = 1e-5
ALPHA = float((2 * LAYERS) ** 0.25)
RING = 4
LEVELS = (64, 32, 16, 8, 4, 2, 1)
WINDOWS = (2, 4, 8, 16)
WIDE, DOWN, HALF = 16, 11, 8
UP_CHUNKS = 2 * KF // 2
DOWN_CHUNKS = 2 * KD

MIX1 = [WIDE] * 18 + [HALF] * 8 + [WIDE] * 4
MIX2 = [WIDE] * 17 + [WIDE, HALF] * 12 + [WIDE] * 4
CROSS = [WIDE] * 2 + [WIDE] * 2 + [WIDE] * 2 + [HALF] * 4
FFN = [WIDE] * UP_CHUNKS + [DOWN] * DOWN_CHUNKS
LAYER1 = FFN + MIX1 + FFN
LAYER2 = FFN + MIX2 + CROSS + FFN


def wide(w):
    n = w.shape[1] // 256
    return w.reshape(8, P, n, 2, P).transpose(2, 1, 3, 0, 4).reshape(n, P, -1)


def half(w):
    n = w.shape[1] // 256
    return w.reshape(4, P, n, 2, P).transpose(2, 1, 3, 0, 4).reshape(n, P, -1)


def down(w):
    return w.reshape(2, 11, P, KD, P).transpose(3, 0, 2, 1, 4).reshape(2 * KD, P, -1)


def moving(w):
    return w.reshape(2, 4, P, 512).transpose(0, 2, 1, 3).reshape(2, P, -1)


def in_turn(a, b):
    return np.stack([a, b], 1).reshape((-1,) + a.shape[1:])


def pack(i):
    out = {WIDE: [], DOWN: [], HALF: []}
    for l in range(LAYERS):
        for f in (1, 2):
            out[WIDE].append(in_turn(wide(i[f"ffn{f}_w_gate"][l]), wide(i[f"ffn{f}_w_up"][l])))
            out[DOWN].append(down(i[f"ffn{f}_w_down"][l]))
            if f == 1:
                w = i["w_in"][l]
                u, q, z, v, og, g0, g1 = (w[:, a:b] for a, b in (
                    (0, 512), (512, 1024), (1024, 1536), (1536, 2048), (2048, 2560), (2560, 3584), (3584, 4608)))
                out[WIDE] += [wide(z), wide(q), moving(v), wide(u), wide(og), wide(g0), wide(g1)]
                out[HALF] += [half(i["w_pool_proj"][l]), half(i["w_hgrn_proj"][l])]
                out[WIDE].append(wide(i["w_out"][l]))
    pack2(i, out)
    return {k: np.ascontiguousarray(np.concatenate(v)) for k, v in out.items()}


def pack2(i, out):
    w = {k[:-2]: v for k, v in i.items() if k.endswith("_2")}
    for l in range(LAYERS):
        for f in range(2):
            if f:
                m = w["w_mix_in"][l]
                at = np.cumsum([0, 512, 128, 512, 64, 8, 512, 512, 512, 512, 512, 512, D, D, D])
                qa, ckv, iq, ik, iw, qs, ks, vs, cb, cc, ch, ga, gb, gc = (m[:, a:b] for a, b in zip(at, at[1:]))
                key = np.concatenate([ik, ik], 1).reshape(8, P, P).transpose(1, 0, 2).reshape(1, P, -1)
                lat = ckv.reshape(8, P, P).transpose(1, 0, 2).reshape(1, P, -1)
                cc, ch, cb = wide(cc), wide(ch), wide(cb)
                conv = np.stack([cc, ch, cb], 1).reshape((6,) + cc.shape[1:])
                out[WIDE] += [wide(iq), np.concatenate([key, lat], 2), wide(qa), conv, wide(qs), wide(ks),
                              moving(vs), wide(gc), wide(ga), wide(gb), wide(w["w_mix_out"][l])]
                out[HALF] += [half(w["w_branch"][l, j]) for j in (2, 0, 1)]
                kv = w["xa_wkv"][l]
                out[WIDE] += [wide(kv[:, :512]), moving(kv[:, 512:]), wide(w["xa_wq"][l])]
                out[HALF].append(half(w["xa_wo"][l]))
            wi = w["ffn_w_in"][l, f]
            out[WIDE].append(in_turn(wide(wi[:, :DFF]), wide(wi[:, DFF:])))
            out[DOWN].append(down(w["ffn_w_out"][l, f]))


def small_weights(i):
    s, j = np.arange(P)[None, :], np.arange(P)[:, None]
    tri = np.concatenate([-(j >= s).astype(np.float32), -np.ones((P, P), np.float32)], 1)
    out = []
    for l in range(LAYERS):
        uk = i["w_uk_2"][l].reshape(4, 2, 64, P).transpose(1, 2, 0, 3).reshape(P, 512)
        uv = i["w_uv_2"][l].transpose(1, 0, 2).reshape(P, 512)
        iw = i["w_mix_in_2"][l][:, 1216:1224].reshape(8, P, 8).transpose(1, 0, 2).reshape(P, 64)
        g = np.broadcast_to(i["kv_norm_g_2"][l], (P, P))
        conv = i["conv_w_2"][l].reshape(3, 4, P).transpose(2, 1, 0).reshape(P, 12)
        bg = i["b_gate_2"][l].reshape(3, 8, P).transpose(2, 0, 1).reshape(P, 24)
        out.append(np.concatenate([uk, uv, iw, g, conv, bg, tri], 1))
    return np.ascontiguousarray(np.stack(out))


def bucket_table():
    n = np.maximum(256 - np.arange(384), 0)
    nf = np.maximum(n, 1).astype(np.float32)
    large = 16 + (np.log(nf / np.float32(16)) / np.float32(np.log(128 / 16)) * np.float32(16)).astype(np.int32)
    b = np.where(n < 16, n, np.minimum(large, 31))
    return (np.arange(32)[:, None] == b[None, :]).astype(np.float32)


def columns(v):
    return np.ascontiguousarray(np.reshape(v, (-1, P)).T)


def constants():
    c = {}
    c["ident"] = np.eye(P, dtype=np.float32)
    s, t = np.arange(P)[:, None], np.arange(P)[None, :]
    lev = [(s // (2 * b) == t // (2 * b)) & (s % (2 * b) < b) & (t % (2 * b) >= b) for b in LEVELS] + [s == t]
    c["levels"] = np.concatenate(lev, 1).astype(np.float32)
    pos = np.arange(1, 17)
    c["counts"] = np.broadcast_to(np.stack([1.0 / np.minimum(pos, w) for w in WINDOWS]).reshape(1, -1),
                                  (P, 64)).astype(np.float32)
    return c


class Chain:

    def __init__(self, eng, sem):
        self.eng, self.sem, self.n, self.turn = eng, sem, 0, 0

    def __call__(self, ins):
        ins.then_inc(self.sem, 1)
        self.n += 1

    def settle(self):
        self.eng.wait_ge(self.sem, self.n + self.turn)


class Turns:

    def __init__(self, kinds):
        self.before, used = [], [0] * RING
        for c, first in enumerate(kinds):
            self.before.append(used[c % RING])
            used[c % RING] += first


def program(nc, t):
    stream = (LAYER1 * 2 + LAYER2 * 2)
    owns, half_done = [], False
    for kind in stream:
        owns.append(kind != DOWN or half_done)
        half_done = kind == DOWN and not half_done
    turns = Turns(owns)
    subs = ["ffn", "mix1", "ffn"] * 2 + ["ffn", "mix2", "cross", "ffn"] * 2
    base = [0]
    for kinds in (FFN, MIX1, FFN) * 2 + (FFN, MIX2, CROSS, FFN) * 2:
        base.append(base[-1] + len(kinds))
    n_subs = len(subs)
    n_norms = n_subs + 1
    n_chunks = base[n_subs]

    with ExitStack() as ctx:
        def sb(name, shape, dt=F32):
            return ctx.enter_context(nc.sbuf_tensor(name, shape, dt))

        def sem(name):
            return ctx.enter_context(nc.semaphore(name))

        raw = sb("raw", [P, RING, WIDE * P])
        w_hi = sb("w_hi", [P, RING, WIDE * P], F32R)
        w_lo = sb("w_lo", [P, RING, WIDE * P], F32R)
        x = sb("x", [P, KD, S])
        x_hi = sb("x_hi", [P, KD, S], F32R)
        x_lo = sb("x_lo", [P, KD, S], F32R)
        with nc.sbuf_tensor("h_parts", [P, 2, KF, S], F32R) as h_parts:
            h_hi, h_lo = h_parts[:, 0], h_parts[:, 1]
        with nc.sbuf_tensor("branches", [P, 2, 12, S], F32R) as branches:
            br_hi, br_lo = branches[:, 0], branches[:, 1]
            with nc.sbuf_tensor("gates", [P, 20, S], F32) as gates:
                pass
            with nc.sbuf_tensor("merged", [P, 2, 8, S], F32R) as merged:
                mg_hi, mg_lo = merged[:, 0], merged[:, 1]
        ctx.enter_context(nc.sbuf_tensor("region", [P, 2, KF, S], F32R))
        tmp = sb("tmp", [P, 44, S])

        ident = sb("ident", [P, P])
        ones = sb("ones", [P, P])
        mean_col = sb("mean_col", [P, 1])
        mean_head = sb("mean_head", [P, 1])
        with nc.sbuf_tensor("levels", [P, len(LEVELS) + 1, P], F32) as levels:
            with nc.sbuf_tensor("pool_w", [P, 4 * P], F32) as pool_w:
                pass
        with nc.sbuf_tensor("small2", [P, 1508], F32) as small2:
            pass
        ctx.enter_context(nc.sbuf_tensor("small_place", [P, 1536], F32))
        counts = sb("counts", [P, 4, 16])
        norm_g = sb("norm_g", [P, 15 * KD])
        norm_b = sb("norm_b", [P, 15 * KD])
        small = sb("small", [P, 32])
        diag = sb("diag", [P, 2 * S])
        sm = sb("sm", [P, 128])
        cols1 = sb("cols1", [P, LAYERS, 3, HEADS1])
        gdummy = sb("gdummy", [P, 1])
        lbc = sb("lbc", [P, 12, HEADS1])

        acc = ctx.enter_context(nc.psum_tensor("acc", [P, RING, 512], F32))
        stat = ctx.enter_context(nc.psum_tensor("stat", [P, 512], F32))
        bc = ctx.enter_context(nc.psum_tensor("bc", [P, 512], F32))
        aux = ctx.enter_context(nc.psum_tensor("aux", [P, 2, 512], F32))

        loaded = [sem(f"loaded{i}") for i in range(RING)]
        hi_done, lo_done, chunk_done = sem("hi_done"), sem("lo_done"), sem("chunk_done")
        acc_taken = [sem(f"acc_taken{i}") for i in range(RING)]
        x_loaded, consts_loaded, consts_set = sem("x_loaded"), sem("consts_loaded"), sem("consts_set")
        y_ready, sq_ready, stat_done, var_ready, sd_ready = (
            sem(n) for n in ("y_ready", "sq_ready", "stat_done", "var_ready", "sd_ready"))
        diag_ready, bc_done, t_ready, xh_ready, x_parts = (
            sem(n) for n in ("diag_ready", "bc_done", "t_ready", "xh_ready", "x_parts"))
        x_new, mixer_loaded, table_chosen = sem("x_new"), sem("mixer_loaded"), sem("table_chosen")
        silu_ready, hid_ready, hid_hi, hid_parts = (
            sem(n) for n in ("silu_ready", "hid_ready", "hid_hi", "hid_parts"))
        v_chain, a_chain, g_chain, p_chain = (sem(n) for n in ("v_chain", "a_chain", "g_chain", "p_chain"))
        out_stored, a_zeroed, pool_w_loaded, x_scaled = (
            sem(n) for n in ("out_stored", "a_zeroed", "pool_w_loaded", "x_scaled"))
        f_ln, k_exp, lb_ready = (sem(n) for n in ("f_ln", "k_exp", "lb_ready"))
        lb_exp, lb_logs = sem("lb_exp"), sem("lb_logs")
        la_d, la_ln, forget_ready = sem("la_d"), sem("la_ln"), sem("forget_ready")
        qog_tanh = sem("qog_tanh")
        pooled_sum, pooled_ready, pool_mixed, pool_hi, pool_parts = (
            sem(n) for n in ("pooled_sum", "pooled_ready", "pool_mixed", "pool_hi", "pool_parts"))
        lev_d, lev_e, lev_q, lev_k, lev_done, lev_taken = (
            sem(n) for n in ("lev_d", "lev_e", "lev_q", "lev_k", "lev_done", "lev_taken"))
        o_done, o_sq, o_stat, o_sd, o_diag, o_bc, ho_ready, ho_hi, ho_parts = (
            sem(n) for n in ("o_done", "o_sq", "o_stat", "o_sd", "o_diag", "o_bc", "ho_ready",
                             "ho_hi", "ho_parts"))
        o_var, o_copied, merged_ready, merged_hi, merged_parts = (
            sem(n) for n in ("o_var", "o_copied", "merged_ready", "merged_hi", "merged_parts"))

        names2 = ("small2_loaded rel_done rel_copied rel_loaded skew_stored bias_loaded iw_done iw_ready gate_bias "
                  "ck_sq ck_var ck_sd ck_ready ck_turned ckf_ready dots_done dots_relu score_ready score_masked "
                  "pen_ready pen_masked lat_done lat_ready "
                  "conv_hi conv_parts log_done log_taken max_ready probs_exp probs_ready "
                  "turned turned_copied ol_done ol_ready ya_done ya_hi ya_parts "
                  "z_done zl_ready sp_ready sp_masked arg_done a_exp a_masked yb_done yb_hi yb_parts "
                  "mg_hi mg_parts").split()
        e = {n: sem(n) for n in names2}
        names3 = "mem_loaded mem_hi mem_parts xl_done xmax_ready x_exp xp_ready xt_done xt_copied xo_done xo_hi xo_parts".split()
        e.update({n: sem(n) for n in names3})
        BIAS = tmp[:, 0:8]
        IQ, QA, QL = tmp[:, 8:12], tmp[:, 16:20], tmp[:, 20:28]
        IK, CKT, CKF, JUNK = tmp[:, 12], tmp[:, 13], tmp[:, 14], tmp[:, 15]
        L1, L0 = tmp[:, 28:36], tmp[:, 36:40]
        SC = tmp[:, 40:42].rearrange("p a b -> p (a b)")[:, 0:384]
        PEN = tmp[:, 42:44].rearrange("p a b -> p (a b)")[:, 0:384]
        R = lambda n: gates[:, 12 + 2 * (n % 2):14 + 2 * (n % 2)].rearrange("p a b -> p (a b)")[:, 0:384]
        QS, KS, VS = gates[:, 0:4], gates[:, 4:8], gates[:, 8:12]
        CC, CZ, CY = gates[:, 16:18], gates[:, 18:20], gates[:, 12:14]
        PT0, PT1, OL = tmp[:, 8:12], tmp[:, 20:28], tmp[:, 28:36]
        SP = lambda n: gates[:, 12 + 2 * (n % 2):14 + 2 * (n % 2)].rearrange("p a b -> p (a b)")[:, 0:384]
        AW = lambda n: gates[:, 16 + 2 * (n % 2):18 + 2 * (n % 2)].rearrange("p a b -> p (a b)")[:, 0:384]
        GT = lambda n: tmp[:, 16 + 2 * (n % 2):18 + 2 * (n % 2)]
        MG = tmp[:, 36:44]
        UK, UV = small2[:, 0:512], small2[:, 512:1024]
        IWW, KVG, CONV, BG = small2[:, 1024:1088], small2[:, 1088:1216], small2[:, 1216:1228], small2[:, 1228:1252]
        NTRI, NONE_ = small2[:, 1252:1380], small2[:, 1380:1508]
        IW, M8, MX, SUM, RIN, CKS = sm[:, 0:16], sm[:, 16:24], sm[:, 24:40], sm[:, 40:56], sm[:, 56:72], sm[:, 72:80]
        XK, XV, XQ = tmp[:, 8:12], tmp[:, 12:16], tmp[:, 16:20]
        XL, XPT = gates[:, 8:16], gates[:, 0:8]
        MEM = [tmp[:, 20:22], tmp[:, 22:24], gates[:, 16:18], gates[:, 18:20]]
        skew = nc.dram_tensor("skew", (8, P * 384), F32, kind="Internal").ap()

        HOT = tmp[0:32, 40:42].rearrange("p a b -> p (a b)")[:, 0:384]
        REL = tmp[0:32, 12:16].rearrange("p a b -> p (a b)")
        STAGE = tmp[:, 0:12].rearrange("p a b -> p (a b)")
        LF, K, Q, V, OG, A2, A = (tmp[:, 4 * j:4 * j + 4] for j in range(7))
        EB, QB, KB = (lambda n, j=j: tmp[:, 28 + 4 * j + 2 * (n % 2):30 + 4 * j + 2 * (n % 2)] for j in range(3))
        T0, T1 = gates[:, 0:8], gates[:, 8:16]
        U, SUM0, SUM1 = gates[:, 8:12], gates[:, 12:16], gates[:, 4:8]
        FA, FL = tmp[:, 28:32], tmp[:, 32:36]
        QT = tmp[:, 36:44]
        HID = lambda j: tmp[:, 20 + 2 * (j % 2):22 + 2 * (j % 2)]
        SIL = lambda j: tmp[:, 16 + 2 * (j % 2):18 + 2 * (j % 2)]
        SQ, T = tmp[:, 24:32], tmp[:, 32:40]

        def flat(ap):
            return ap.rearrange("p a b -> p (a b)")


        def split_hi(act, c, slot, kind, turn=0, used=0):
            act.wait_ge(loaded[slot], 16 * (c // RING + 1) + turn * 16)
            if c >= RING:
                act.wait_ge(chunk_done, c - RING + 1 + used)
            n = kind * P
            nc.scalar.activation(w_hi[:, slot, 0:n], raw[:, slot, 0:n], ACT.Copy).then_inc(hi_done, 1)

        def split_lo(dve, c, slot, kind, turn=0, used=0):
            dve.wait_ge(hi_done, c + 1 + used)
            n = kind * P
            nc.vector.tensor_tensor(w_lo[:, slot, 0:n], raw[:, slot, 0:n], w_hi[:, slot, 0:n].bitcast(F32),
                                    ALU.subtract).then_inc(lo_done, 1)

        class Ahead:

            def __init__(self, eng, split):
                self.eng, self.split, self.next = eng, split, 0

            def to(self, c):
                while self.next <= min(c, n_chunks - 1):
                    self.split(self.eng, self.next, self.next % RING, stream[self.next])
                    self.next += 1

        block = ctx.enter_context(nc.Block())

        @block.sync
        def _(sp):
            sp.dma_start(flat(x), t["x"]).then_inc(x_loaded, 16)
            sp.dma_start(ident[:, :], t["ident"]).then_inc(consts_loaded, 16)
            sp.dma_start(norm_g[:, :], t["norm_g"]).then_inc(consts_loaded, 16)
            place = {WIDE: 0, DOWN: 0, HALF: 0}
            c = 0
            while c < n_chunks:
                kind, k = stream[c], 1
                while c + k < n_chunks and stream[c + k] == kind:
                    k += 1
                w, at = t[f"w{kind}"], place[kind]

                def load(j, src, turn=0):
                    slot = (c + j) % RING
                    if c + j >= RING:
                        sp.wait_ge(lo_done, c + j - RING + 1 + RING * turn)
                    sp.dma_start(raw[:, slot, 0:kind * P], src).then_inc(loaded[slot], 16)

                first = RING if c == 0 else 0
                for j in range(first):
                    load(j, w[at + j])
                if c == 0:
                    sp.dma_start(flat(levels), t["levels"]).then_inc(mixer_loaded, 16)
                    sp.dma_start(flat(counts), t["counts"]).then_inc(mixer_loaded, 16)
                    sp.dma_start(cols1[:].rearrange("p a b c -> p (a b c)"), t["cols1"]).then_inc(mixer_loaded, 16)
                    sp.dma_start(norm_b[:, :], t["norm_b"]).then_inc(mixer_loaded, 16)
                rounds = (k - first) // RING
                if rounds > 1:
                    with sp.Fori(0, rounds) as i:
                        for j in range(RING):
                            load(first + j, w[i * RING + (at + first + j)], i)
                else:
                    rounds = 0
                for j in range(first + rounds * RING, k):
                    load(j, w[at + j])
                c += k
                place[kind] += k
            sp.wait_ge(x_new, KD * (n_norms - 6))
            sp.dma_start(t["out"], flat(x)).then_inc(out_stored, 16)
            sp.wait_ge(out_stored, 16)

        def y_event(N, n):
            if N == 0:
                return x_loaded, 16
            end = base[N]
            c = end - 2 * (KD - n) + 1 if subs[N - 1] == "ffn" else end - KD // 2 + n // 2
            return acc_taken[c % RING], turns.before[c] + 1

        def replaces(N):
            return N >= 6

        def parts(N):
            return N < n_subs

        def centred(N):
            return N >= 7

        @block.tensor
        def _(pe):

            def mm3(out, w_hi_, w_lo_, v_hi_, v_lo_, start, stop):
                nc.tensor.matmul(out, w_hi_, v_hi_, start=start, stop=False)
                nc.tensor.matmul(out, w_hi_, v_lo_, start=False, stop=False)
                return nc.tensor.matmul(out, w_lo_, v_hi_, start=False, stop=stop)

            def chunk_ready(c, used=0, bank=None, turn=0):
                pe.wait_ge(lo_done, c + 1 + used)
                if bank is not None and turns.before[bank]:
                    pe.wait_ge(acc_taken[bank % RING], turns.before[bank] + turn)

            def wblock(slot, b, width=P):
                return w_hi[:, slot, b * width:(b + 1) * width], w_lo[:, slot, b * width:(b + 1) * width]

            def two_tiles(c, kt, src_hi, src_lo, used=0, turn=0, wait_k=None):
                chunk_ready(c, used, c, turn)
                slot = c % RING
                for tl in range(2):
                    for k in range(kt):
                        if tl == 0 and wait_k is not None:
                            wait_k(k)
                        last = mm3(acc[:, slot, tl * S:(tl + 1) * S], *wblock(slot, tl * kt + k),
                                   src_hi[:, k], src_lo[:, k], k == 0, k == kt - 1)
                last.then_inc(chunk_done, 1)

            def token_major(c):
                for half_ in range(2):
                    chunk_ready(c + half_, 0, c + half_)
                    if half_ == 0:
                        pe.wait_ge(acc_taken[(c + 1) % RING], turns.before[c + 1])
                    for tt in range(2):
                        for k in range(4):
                            kk = 4 * half_ + k
                            xh, xl = (v[:, kk, tt * P:(tt + 1) * P] for v in (x_hi, x_lo))
                            wh, wl = wblock((c + half_) % RING, k, 512)
                            out = acc[:, (c + tt) % RING, :]
                            nc.tensor.matmul(out, xh, wh, start=kk == 0, stop=False)
                            nc.tensor.matmul(out, xl, wh, start=False, stop=False)
                            last = nc.tensor.matmul(out, xh, wl, start=False, stop=kk == 7)
                    last.then_inc(chunk_done, 1)

            def norm(N):
                for n in range(KD):
                    pe.wait_ge(sq_ready, KD * N + n + 1)
                    for tt in range(2):
                        if centred(N):
                            nc.tensor.matmul(stat[:, 2 * tt:2 * tt + 1], x[:, n, tt * P:(tt + 1) * P], mean_col[:, :],
                                             start=n == 0 and tt == 0, stop=n == 7, skip_group_check=True)
                        last = nc.tensor.matmul(stat[:, 2 * tt + 1:2 * tt + 2], SQ[:, n, tt * P:(tt + 1) * P],
                                                mean_col[:, :], start=n == 0 and tt == 0 and not centred(N),
                                                stop=n == 7, skip_group_check=True)
                last.then_inc(stat_done, 1)
                is_cross = N < n_subs and subs[N] == "cross"
                if is_cross:
                    memory_keys(N, subs[:N].count("cross"), 0)
                width = 2 * S if centred(N) else S
                pe.wait_ge(diag_ready, N + 1)
                nc.tensor.matmul(bc[:, 0:width], ones[:, :], diag[:, 0:width], start=True, stop=True).then_inc(bc_done, 1)
                if is_cross:
                    memory_keys(N, subs[:N].count("cross"), 1)
                    memory_values(N)

            def ffn(s, f):
                c0 = base[s]

                def x_part(k):
                    pe.wait_ge(x_parts, KD * s + k + 1)

                first = 0 if s else RING
                for j in range(first):
                    two_tiles(c0 + j, 8, x_hi, x_lo, wait_k=x_part if j == 0 else None)
                with pe.Fori(0, 5 - first // RING) as i:
                    for j in range(first, first + RING):
                        two_tiles(c0 + j, 8, x_hi, x_lo, used=4 * i, turn=i, wait_k=x_part if j == 0 else None)
                for j in range(20, 22):
                    two_tiles(c0 + j, 8, x_hi, x_lo)
                if s == 6:
                    bias_rows()
                c1 = c0 + UP_CHUNKS
                with pe.Fori(0, 4) as i:
                    for j in range(4):
                        c = c1 + j
                        own = c1 + j + 1 - j % 2
                        chunk_ready(c, 4 * i, own if j % 2 == 0 else None, i)
                        for k in range(11):
                            kk = 11 * (j % 2) + k
                            if k == 0 or kk % 2 == 0:
                                pe.wait_ge(hid_parts, 11 * f + kk // 2 + 1)
                            last = mm3(acc[:, own % RING, 0:S], *wblock(c % RING, k), h_hi[:, kk], h_lo[:, kk],
                                       kk == 0, kk == KF - 1)
                        last.then_inc(chunk_done, 1)

            def mix1(s, l):
                c0 = base[s]

                def x_part(k):
                    pe.wait_ge(x_parts, KD * s + k + 1)

                for j in range(4):
                    two_tiles(c0 + j, 8, x_hi, x_lo, wait_k=x_part if j == 0 else None)
                token_major(c0 + 4)
                for j in range(6, 10):
                    two_tiles(c0 + j, 8, x_hi, x_lo)

                def unit(n):
                    li, hp = UNITS[n]
                    if n >= 2:
                        pe.wait_ge(lev_taken, 18 * l + n - 1)
                    if li == 7:
                        if n == 0:
                            pe.wait_ge(forget_ready, 1 + 2 * l + 1)
                            pe.wait_ge(pool_parts, 4 * (l + 1))
                        kb, qb = K[:, 2 * hp:2 * hp + 2], Q[:, 2 * hp:2 * hp + 2]
                    else:
                        pe.wait_ge(lev_q, 16 * l + n - 2 + 1)
                        pe.wait_ge(lev_k, 16 * l + n - 2 + 1)
                        kb, qb = KB(n), QB(n)
                    out = aux[:, n % 2, :]
                    for hh in range(2):
                        for b in range(2):
                            if li == 8:
                                if b == 0:
                                    last = nc.tensor.matmul(out[:, hh * P:(hh + 1) * P], kb[:, hh, 0:P],
                                                            qb[:, hh, P:2 * P], start=True, stop=True)
                            else:
                                col = (2 * hh + b) * P
                                last = nc.tensor.matmul(out[:, col:col + P], kb[:, hh, b * P:(b + 1) * P],
                                                        qb[:, hh, b * P:(b + 1) * P], start=True, stop=True)
                    last.then_inc(lev_done, 1)

                two_tiles(c0 + 10, 8, x_hi, x_lo)
                pe.wait_ge(pooled_ready, l + 1)
                for g in range(4):
                    last = nc.tensor.matmul(aux[:, g // 2, (g % 2) * S:(g % 2 + 1) * S], pool_w[:, g * P:(g + 1) * P],
                                            U[:, g], start=True, stop=True)
                    if g % 2:
                        last.then_inc(pool_mixed, 1)
                for j in range(8):
                    if j:
                        two_tiles(c0 + 10 + j, 8, x_hi, x_lo)
                    unit(2 * j)
                    unit(2 * j + 1)
                unit(16)
                unit(17)
                two_tiles(c0 + 18, 4, br_hi, br_lo)
                pe.wait_ge(lev_taken, 18 * (l + 1))
                for h in range(HEADS1):
                    for b in range(2):
                        out = aux[:, h // 2, (h % 2) * S + b * P:(h % 2) * S + (b + 1) * P]
                        last = nc.tensor.matmul(out, V[:, 2 * b:2 * b + 2].rearrange("p a c -> p (a c)")[:, h * P:(h + 1) * P],
                                                A[:, h, b * P:(b + 1) * P], start=True, stop=b == 0)
                        if b:
                            last = nc.tensor.matmul(out, V[:, 0:2].rearrange("p a c -> p (a c)")[:, h * P:(h + 1) * P],
                                                    A2[:, h // 2, (h % 2) * P:(h % 2 + 1) * P], start=False, stop=True)
                    if h % 2:
                        last.then_inc(o_done, 1)
                two_tiles(c0 + 19, 4, br_hi, br_lo)
                pe.wait_ge(o_sq, 2 * (l + 1))
                for h in range(HEADS1):
                    for b in range(2):
                        last = nc.tensor.matmul(stat[:, 2 * h + b:2 * h + b + 1], QT[:, h, b * P:(b + 1) * P],
                                                mean_head[:, :], start=h == 0 and b == 0, stop=True, skip_group_check=True)
                last.then_inc(o_stat, 1)
                two_tiles(c0 + 20, 4, br_hi, br_lo)
                two_tiles(c0 + 21, 4, br_hi, br_lo)
                pe.wait_ge(o_diag, l + 1)
                for p in range(2):
                    nc.tensor.matmul(aux[:, p, :], ones[:, :], flat(QT[:, 4 + 2 * p:6 + 2 * p]),
                                     start=True, stop=True).then_inc(o_bc, 1)
                for j in range(4):
                    if j == 0:
                        def ho_part(k):
                            pe.wait_ge(ho_parts, 2 * l + k // 2 + 1)
                    two_tiles(c0 + 22 + j, 4, br_hi[:, 4:8], br_lo[:, 4:8], wait_k=ho_part if j == 0 else None)

                def merged_part(k):
                    pe.wait_ge(merged_parts, 4 * l + k // 2 + 1)
                for j in range(4):
                    two_tiles(c0 + 26 + j, 8, x_hi, x_lo, wait_k=merged_part if j == 0 else None)

            def bias_rows():
                pe.wait_ge(e["rel_loaded"], 32)
                for h in range(8):
                    if h >= 2:
                        pe.wait_ge(e["rel_copied"], h - 1)
                    nc.tensor.matmul(aux[:, h % 2, 0:384], REL[:, h * P:(h + 1) * P], HOT, start=True,
                                     stop=True).then_inc(e["rel_done"], 1)

            def mix2(s, l):
                c0 = base[s]

                def x_part(k):
                    pe.wait_ge(x_parts, KD * s + k + 1)

                two_tiles(c0, 8, x_hi, x_lo, wait_k=x_part)
                two_tiles(c0 + 1, 8, x_hi, x_lo)
                c = c0 + 2
                chunk_ready(c, 0, c)
                for k in range(8):
                    mm3(acc[:, c % RING, 0:S], *wblock(c % RING, k), x_hi[:, k], x_lo[:, k], k == 0, k == 7)
                for tt in range(2):
                    for k in range(8):
                        wh, wl = wblock(c % RING, 8 + k)
                        xh, xl = (v[:, k, tt * P:(tt + 1) * P] for v in (x_hi, x_lo))
                        out = acc[:, c % RING, S + tt * P:S + (tt + 1) * P]
                        nc.tensor.matmul(out, xh, wh, start=k == 0, stop=False)
                        nc.tensor.matmul(out, xl, wh, start=False, stop=False)
                        last = nc.tensor.matmul(out, xh, wl, start=False, stop=k == 7)
                last.then_inc(chunk_done, 1)
                pe.wait_ge(e["small2_loaded"], 16 * (l + 1))
                for tt in range(2):
                    for k in range(8):
                        last = nc.tensor.matmul(stat[:, 8 * tt:8 * tt + 8], x[:, k, tt * P:(tt + 1) * P],
                                                IWW[:, 8 * k:8 * k + 8], start=k == 0, stop=k == 7)
                last.then_inc(e["iw_done"], 1)
                two_tiles(c0 + 3, 8, x_hi, x_lo)
                for q in (c0, c0 + 1, c0 + 2):
                    pe.wait_ge(acc_taken[q % RING], turns.before[q] + 1)
                for h in range(8):
                    if h >= 2:
                        pe.wait_ge(e["dots_relu"], 8 * l + h - 1)
                    r = slice(64 * (h % 2), 64 * (h % 2) + 64)
                    nc.tensor.matmul(aux[:, h % 2, 0:P], IQ[r, h // 2, 0:P], IK[r, 0:P], start=True, stop=True)
                    nc.tensor.matmul(aux[:, h % 2, P:3 * P], IQ[r, h // 2, P:S], IK[r, :], start=True,
                                     stop=True).then_inc(e["dots_done"], 1)
                two_tiles(c0 + 4, 8, x_hi, x_lo)
                pe.wait_ge(e["ck_ready"], l + 1)
                pe.wait_ge(e["dots_relu"], 8 * (l + 1))
                for tt in range(2):
                    last = nc.tensor.transpose(aux[:, 0, tt * P:(tt + 1) * P], CKT[:, tt * P:(tt + 1) * P], ident[:, :])
                last.then_inc(e["ck_turned"], 1)
                two_tiles(c0 + 5, 8, x_hi, x_lo)
                for q in (c0 + 3, c0 + 4):
                    pe.wait_ge(acc_taken[q % RING], turns.before[q] + 1)
                pe.wait_ge(e["ckf_ready"], l + 1)
                for h in range(8):
                    r = slice(64 * (h % 2), 64 * (h % 2) + 64)
                    if h in (4, 5):
                        pe.wait_ge(e["lat_ready"], 4 * l + h - 3)
                    last = nc.tensor.matmul(aux[:, h % 2, (h // 2 % 2) * S:(h // 2 % 2 + 1) * S], UK[r, (h // 2) * P:(h // 2 + 1) * P],
                                            QA[r, h // 2], start=True, stop=True)
                    if h % 4 >= 2:
                        last.then_inc(e["lat_done"], 1)
                for j in range(6, 15):
                    two_tiles(c0 + j, 8, x_hi, x_lo)
                pe.wait_ge(e["lat_ready"], 4 * (l + 1))
                for n in range(6):
                    if n >= 2:
                        pe.wait_ge(e["log_taken"], 6 * l + n - 1)
                    if n < 4:
                        for hh in range(2):
                            last = nc.tensor.matmul(aux[:, n % 2, hh * S:(hh + 1) * S], QL[:, 2 * n + hh, P:S], CKF[:, :],
                                                    start=True, stop=True)
                    else:
                        for hh in range(4):
                            last = nc.tensor.matmul(aux[:, n % 2, hh * P:(hh + 1) * P], QL[:, 4 * (n - 4) + hh, 0:P],
                                                    CKF[:, 0:P], start=True, stop=True)
                    last.then_inc(e["log_done"], 1)
                token_major(c0 + 15)

                def turn(n):
                    pe.wait_ge(e["turned_copied" if n >= 2 else "log_taken"], 6 * l + n - 1 if n >= 2 else 6 * (l + 1))
                    for q in range(4):
                        src = L0[:, 2 * n:2 * n + 2].rearrange("p a b -> p (a b)")[:, q * P:(q + 1) * P] if n < 2 else \
                            L1[:, 2 * (n - 2) + q // 2, (q % 2) * P:(q % 2 + 1) * P]
                        last = nc.tensor.transpose(aux[:, n % 2, q * P:(q + 1) * P], src, ident[:, :])
                    last.then_inc(e["turned"], 1)

                def z(h):
                    if h == 0:
                        for q in range(11, 17):
                            pe.wait_ge(acc_taken[(c0 + q) % RING], turns.before[c0 + q] + 1)
                        pe.wait_ge(e["ya_parts"], 2 * (l + 1))
                    if h >= 2:
                        pe.wait_ge(e["sp_ready"], 8 * l + h - 1)
                    r = slice(64 * (h % 2), 64 * (h % 2) + 64)
                    nc.tensor.matmul(aux[:, h % 2, 0:S], KS[r, h // 2, 0:P], QS[r, h // 2, :], start=True, stop=True)
                    nc.tensor.matmul(aux[:, h % 2, S:384], KS[r, h // 2, P:S], QS[r, h // 2, P:S], start=True,
                                     stop=True).then_inc(e["z_done"], 1)

                def arg(h):
                    out = (stat, bc)[h % 2]
                    if h >= 2:
                        pe.wait_ge(e["yb_parts"], 8 * l + h - 1)
                    pe.wait_ge(e["sp_masked"], 8 * l + h + 1)
                    r = slice(64 * (h % 2), 64 * (h % 2) + 64)
                    sp = SP(h)
                    kw = dict(skip_group_check=True)
                    nc.tensor.matmul(out[:, 0:S], KS[r, h // 2, 0:P], QS[r, h // 2, :], start=True, stop=False, **kw)
                    nc.tensor.matmul(out[:, S:384], KS[r, h // 2, P:S], QS[r, h // 2, P:S], start=False, stop=False, **kw)
                    nc.tensor.matmul(out[:, 0:S], NTRI, sp[:, 0:S], start=False, stop=False, **kw)
                    nc.tensor.matmul(out[:, P:S], NONE_, sp[:, S:384], start=False, stop=False, **kw)
                    nc.tensor.matmul(out[:, S:384], NTRI, sp[:, S:384], start=False, stop=True, **kw).then_inc(e["arg_done"], 1)

                def weigh(h):
                    out = (stat, bc)[h % 2][64 * (h % 2):64 * (h % 2) + 64, :]
                    pe.wait_ge(e["a_masked"], 8 * l + h + 1)
                    v = [flat(VS[:, 2 * tt:2 * tt + 2])[:, 64 * h:64 * h + 64] for tt in range(2)]
                    kw = dict(skip_group_check=True)
                    nc.tensor.matmul(out[:, 0:S], v[0], AW(h)[:, 0:S], start=True, stop=False, **kw)
                    nc.tensor.matmul(out[:, P:S], v[1], AW(h)[:, S:384], start=False, stop=True, **kw).then_inc(e["yb_done"], 1)

                def gate(n):
                    two_tiles(c0 + 17 + 2 * n, 8, x_hi, x_lo)

                def branch(n, wait_k=None):
                    at = (8, 0, 4)[n // 4]
                    two_tiles(c0 + 18 + 2 * n, 4, br_hi[:, at:at + 4], br_lo[:, at:at + 4], wait_k=wait_k)

                gate(0)
                pe.wait_ge(e["probs_ready"], 2 * l + 1)
                turn(0)
                turn(1)
                pe.wait_ge(e["probs_ready"], 2 * l + 2)
                for n in range(2, 6):
                    turn(n)
                branch(0, lambda k: pe.wait_ge(e["conv_parts"], 2 * l + k // 2 + 1))
                pe.wait_ge(e["turned_copied"], 6 * (l + 1))
                for n in range(4):
                    if n >= 2:
                        pe.wait_ge(e["ol_ready"], 4 * l + n - 1)
                    g = n % 2
                    if n < 2:
                        last = nc.tensor.matmul(aux[:, g, :], CKT[:, 0:P], flat(PT0[:, 2 * g:2 * g + 2]), start=True, stop=True)
                    else:
                        for tt in range(2):
                            rhs = PT1[:, 4 * g:4 * g + 4].rearrange("p h (s t) -> p h s t", s=2)[:, :, tt]
                            last = nc.tensor.matmul(aux[:, g, :], CKT[:, tt * P:(tt + 1) * P], rhs, start=tt == 0, stop=tt == 1)
                    last.then_inc(e["ol_done"], 1)
                gate(1)
                pe.wait_ge(e["ol_ready"], 4 * (l + 1))
                for h in range(8):
                    out = aux[64 * (h % 2):64 * (h % 2) + 64, h // 4, (h // 2 % 2) * S:(h // 2 % 2 + 1) * S]
                    last = nc.tensor.matmul(out, UV[:, 64 * h:64 * h + 64], OL[:, h], start=True, stop=True)
                    if h % 4 == 3:
                        last.then_inc(e["ya_done"], 1)
                branch(1)
                def step(q):
                    if q % 2 == 0:
                        gate(2 + q // 2)
                    elif q == 5:
                        branch(4, lambda k: pe.wait_ge(e["ya_parts"], 2 * l + k // 2 + 1))
                    else:
                        branch(2 + q // 2)

                z(0)
                for h in range(8):
                    step(h)
                    if h < 7:
                        z(h + 1)
                    arg(h)
                    if h:
                        weigh(h - 1)
                step(8)
                weigh(7)
                for q in range(9, 12):
                    step(q)
                for n in range(8, 12):
                    gate(n)
                    branch(n, (lambda k: pe.wait_ge(e["yb_parts"], 8 * l + 2 * k + 2)) if n == 8 else None)
                for j in range(4):
                    two_tiles(c0 + 41 + j, 8, mg_hi, mg_lo,
                              wait_k=(lambda k: pe.wait_ge(e["mg_parts"], 4 * l + k // 2 + 1)) if j == 0 else None)

            def memory_keys(s, l, j):
                two_tiles(base[s] + j, 8, br_hi, br_lo,
                          wait_k=(lambda k: pe.wait_ge(e["mem_parts"], 4 * l + k // 2 + 1)) if j == 0 else None)

            def memory_values(s):
                c0 = base[s]
                for half_ in range(2):
                    for tt in range(2):
                        if half_ == 0:
                            chunk_ready(c0 + 2, 0, c0 + 2 + tt)
                    chunk_ready(c0 + 2 + half_)
                    for tt in range(2):
                        for k in range(4):
                            kk = 4 * half_ + k
                            wh, wl = wblock((c0 + 2 + half_) % RING, k, 512)
                            out = acc[:, (c0 + 2 + tt) % RING, :]
                            nc.tensor.matmul(out, br_hi[:, kk, tt * P:(tt + 1) * P], wh, start=kk == 0, stop=False)
                            nc.tensor.matmul(out, br_lo[:, kk, tt * P:(tt + 1) * P], wh, start=False, stop=False)
                            last = nc.tensor.matmul(out, br_hi[:, kk, tt * P:(tt + 1) * P], wl, start=False, stop=kk == 7)
                    last.then_inc(chunk_done, 1)

            def cross(s, l):
                c0 = base[s]
                for j in range(2):
                    two_tiles(c0 + 4 + j, 8, x_hi, x_lo,
                              wait_k=(lambda k: pe.wait_ge(x_parts, KD * s + k + 1)) if j == 0 else None)
                for q in range(6):
                    pe.wait_ge(acc_taken[(c0 + q) % RING], turns.before[c0 + q] + 1)
                banks = [aux[:, 0, :], aux[:, 1, :], stat[:, :], bc[:, :]]
                for n in range(4):
                    for hh in range(2):
                        h = 2 * (n % 2) + hh
                        last = nc.tensor.matmul(banks[n][:, hh * S:(hh + 1) * S], XQ[:, h, (n // 2) * P:(n // 2 + 1) * P],
                                                XK[:, h, :], start=True, stop=True)
                    last.then_inc(e["xl_done"], 1)
                for n in range(4):
                    pe.wait_ge(e["xp_ready"], 4 * l + n + 1)
                    for q in range(4):
                        src = XL[:, 2 * n + q // 2, (q % 2) * P:(q % 2 + 1) * P]
                        last = nc.tensor.transpose(banks[n][:, q * P:(q + 1) * P], src, ident[:, :])
                    last.then_inc(e["xt_done"], 1)
                pe.wait_ge(e["xt_copied"], 4 * (l + 1))
                for h in range(4):
                    for tt in range(2):
                        rhs = XPT.rearrange("p (b h) (s t) -> p h s b t", b=2, s=2)[:, h, tt]
                        last = nc.tensor.matmul(aux[:, h // 2, (h % 2) * S:(h % 2 + 1) * S],
                                                flat(XV[:, 2 * tt:2 * tt + 2])[:, h * P:(h + 1) * P], rhs,
                                                start=tt == 0, stop=tt == 1)
                    if h % 2:
                        last.then_inc(e["xo_done"], 1)
                for j in range(4):
                    two_tiles(c0 + 6 + j, 4, br_hi[:, 8:12], br_lo[:, 8:12],
                              wait_k=(lambda k: pe.wait_ge(e["xo_parts"], 2 * l + k // 2 + 1)) if j == 0 else None)

            pe.wait_ge(consts_loaded, 16 * N_CONSTS)
            pe.wait_ge(consts_set, 3)
            for N in range(n_norms):
                norm(N)
                if N < n_subs:
                    if subs[N] == "ffn":
                        ffn(N, subs[:N].count("ffn"))
                    if subs[N] == "mix1":
                        mix1(N, subs[:N].count("mix1"))
                    if subs[N] == "mix2":
                        mix2(N, subs[:N].count("mix2"))
                    if subs[N] == "cross":
                        cross(N, subs[:N].count("cross"))

        @block.scalar
        def _(act):
            ac = Chain(act, a_chain)
            ahead = Ahead(act, split_hi)

            def square(N, n, turn=0, width=1, wait_turn=0):
                ev, val = y_event(N, n)
                act.wait_ge(ev, val + wait_turn)
                nc.scalar.activation(SQ[:, n:n + width] if isinstance(turn, int) else SQ[:, bass.ds(n + turn, 1)],
                                     x[:, n:n + width] if isinstance(turn, int) else x[:, bass.ds(n + turn, 1)],
                                     ACT.Square).then_inc(sq_ready, width)

            def choose_sqrt():
                if choices:
                    act.wait_ge(table_chosen, len(choices))
                choices.append(1)
                nc.scalar.activation(small[:, 31:32], mean_col[:, :], ACT.Sqrt).then_inc(table_chosen, 1)

            choices = []

            def norm(N):
                act.wait_ge(var_ready, N + 1)
                nc.scalar.activation(small[:, 2:4], small[:, 0:2], ACT.Sqrt).then_inc(sd_ready, 1)
                if N == 0:
                    ahead.to(0)
                for n in range(KD):
                    act.wait_ge(t_ready, KD * N + n + 1)
                    g = norm_g[:, KD * N + n:KD * N + n + 1]
                    if replaces(N):
                        nc.scalar.activation(x[:, n], T[:, n], ACT.Identity, scale=g,
                                             bias=norm_b[:, KD * N + n:KD * N + n + 1]).then_inc(x_new, 1)
                        if parts(N):
                            act.wait_ge(x_new, KD * (N - 6) + n + 1)
                            nc.scalar.activation(x_hi[:, n], x[:, n], ACT.Copy).then_inc(xh_ready, 1)
                    else:
                        nc.scalar.activation(x_hi[:, n], T[:, n], ACT.Copy, scale=g).then_inc(xh_ready, 1)

            def ffn(s, f):
                c0 = base[s]

                def pair(i, p, turn=0):
                    g = c0 + 2 * p
                    act.wait_ge(chunk_done, g + 1 + 4 * turn)
                    nc.scalar.activation(flat(SIL(p)), acc[:, g % RING, :], ACT.Silu).then_inc(acc_taken[g % RING], 1)
                    yield 0
                    act.wait_ge(acc_taken[(g + 1) % RING], turns.before[g + 1] + 1 + turn)
                    at = bass.ds(2 * p + 4 * turn, 2)
                    nc.scalar.activation(h_hi[:, at], HID(p), ACT.Copy).then_inc(hid_hi, 1)
                    yield 1

                with act.Fori(0, 4) as i:
                    for p in range(2):
                        for u in pair(i, p, i):
                            c = c0 + 2 * p + u
                            split_hi(act, c + 4, c % RING, WIDE, turn=i, used=4 * i)
                ahead.next = c0 + 20
                for p in range(8, 11):
                    for u in pair(0, p):
                        ahead.to(c0 + 2 * p + u + 4)
                if s == 6:
                    bias_rows()
                choose_sqrt()
                c1 = c0 + UP_CHUNKS
                with act.Fori(0, 3) as i:
                    for n in range(2):
                        square(s + 1, n, turn=2 * i, wait_turn=i)
                        for u in range(2):
                            c = c1 + 2 * n + u
                            split_hi(act, c + 4, c % RING, DOWN, turn=i, used=4 * i)
                ahead.next = c1 + 16
                if s == 6:
                    act.wait_ge(e["skew_stored"], 16)
                    act.dma_start(BIAS, skew[:, P:P + P * 383].rearrange("h (p w) -> p h w", w=383)[:, :, 0:S])\
                        .then_inc(e["bias_loaded"], 16)
                for n in range(6, 8):
                    square(s + 1, n)
                    ahead.to(c1 + 2 * n + 1 + 4)

            def mix1(s, l):
                c0 = base[s]
                act.wait_ge(mixer_loaded, 16 * N_MIXER)
                if l:
                    act.wait_ge(lb_ready, 1)
                    nc.scalar.activation(lbc[:, 2:4], lbc[:, 2:4], ACT.Exp).then_inc(lb_exp, 1)
                    act.wait_ge(lb_ready, 2)
                    nc.scalar.activation(lbc[:, 8:10], lbc[:, 8:10], ACT.Ln).then_inc(lb_logs, 1)
                for p in range(2):
                    ahead.to(c0 + p + 4)
                    act.wait_ge(chunk_done, c0 + p + 1)
                    ac(nc.scalar.activation(flat(FL[:, 2 * p:2 * p + 2]), acc[:, (c0 + p) % RING, :], ACT.Abs))
                    ac.settle()
                    ac(nc.scalar.activation(FL[:, 2 * p:2 * p + 2], FL[:, 2 * p:2 * p + 2], ACT.Exp, scale=-1.0))
                    ac.settle()
                    nc.scalar.activation(FL[:, 2 * p:2 * p + 2], FL[:, 2 * p:2 * p + 2], ACT.Ln, bias=1.0).then_inc(f_ln, 1)
                    b = (c0 + p) % RING
                    act.wait_ge(acc_taken[b], turns.before[c0 + p] + 1)
                    nc.scalar.activation(K[:, 2 * p:2 * p + 2], FA[:, 2 * p:2 * p + 2], ACT.Exp, scale=-1.0).then_inc(k_exp, 1)
                    if l:
                        act.wait_ge(la_d, p + 1)
                        ac(nc.scalar.activation(FL[:, 2 * p:2 * p + 2], FA[:, 2 * p:2 * p + 2], ACT.Abs))
                        ac.settle()
                        ac(nc.scalar.activation(FL[:, 2 * p:2 * p + 2], FL[:, 2 * p:2 * p + 2], ACT.Exp, scale=-1.0))
                        ac.settle()
                        nc.scalar.activation(FL[:, 2 * p:2 * p + 2], FL[:, 2 * p:2 * p + 2], ACT.Ln, bias=1.0).then_inc(la_ln, 1)
                for p in range(2):
                    c = c0 + 2 + p
                    act.wait_ge(chunk_done, c + 1)
                    nc.scalar.activation(flat(QT[:, 2 * p:2 * p + 2]), acc[:, c % RING, :], ACT.Tanh, scale=0.5).then_inc(qog_tanh, 1)
                    ahead.to(c + 4)
                act.wait_ge(chunk_done, c0 + 5 + 1)
                for tt in range(2):
                    c = c0 + 4 + tt
                    nc.scalar.activation(flat(V[:, 2 * tt:2 * tt + 2]), acc[:, c % RING, :], ACT.Copy, scale=0.5).then_inc(acc_taken[c % RING], 1)
                ahead.to(c0 + 5 + 4)
                for p in range(2):
                    c = c0 + 6 + p
                    act.wait_ge(chunk_done, c + 1)
                    nc.scalar.activation(flat(U[:, 2 * p:2 * p + 2]), acc[:, c % RING, :], ACT.Copy).then_inc(acc_taken[c % RING], 1)
                    ahead.to(c + 4)
                for p in range(2):
                    c = c0 + 8 + p
                    act.wait_ge(chunk_done, c + 1)
                    nc.scalar.activation(flat(QT[:, 4 + 2 * p:6 + 2 * p]), acc[:, c % RING, :], ACT.Tanh, scale=0.5).then_inc(qog_tanh, 1)
                    ahead.to(c + 4)
                def gate(j):
                    c = c0 + 10 + j
                    act.wait_ge(chunk_done, c + 1)
                    to = (T0 if j < 4 else T1)[:, 2 * (j % 4):2 * (j % 4) + 2]
                    if j == 4:
                        act.wait_ge(pool_mixed, 2 * (l + 1))
                    nc.scalar.activation(flat(to), acc[:, c % RING, :], ACT.Tanh, scale=0.5).then_inc(acc_taken[c % RING], 1)
                    ahead.to(c + 4)

                gate(0)
                for g in range(4):
                    act.wait_ge(pool_mixed, 2 * l + g // 2 + 1)
                    nc.scalar.activation(br_hi[:, g], aux[:, g // 2, (g % 2) * S:(g % 2 + 1) * S], ACT.Copy,
                                         scale=cols1[:, l, 0, g:g + 1]).then_inc(pool_hi, 1)

                def decay(n):
                    if n < 2 or n > 17:
                        return
                    act.wait_ge(lev_d, 16 * l + n - 1)
                    ac(nc.scalar.activation(flat(EB(n)), flat(EB(n)), ACT.Abs))
                    ac.settle()
                    nc.scalar.activation(flat(EB(n)), flat(EB(n)), ACT.Exp, scale=-1.0).then_inc(lev_e, 1)

                for j in range(8):
                    decay(2 * j + 1)
                    decay(2 * j + 2)
                    if j:
                        gate(j)
                decay(17)
                ahead.to(c0 + 18 + 4)
                for p in range(2):
                    act.wait_ge(o_done, 2 * l + p + 1)
                    nc.scalar.activation(flat(QT[:, 2 * p:2 * p + 2]), aux[:, p, :], ACT.Square).then_inc(o_sq, 1)
                ahead.to(c0 + 19 + 4)
                act.wait_ge(o_var, l + 1)
                nc.scalar.activation(small[:, 16:24], small[:, 8:16], ACT.Sqrt).then_inc(o_sd, 1)
                ahead.to(c0 + 21 + 4)
                for p in range(2):
                    act.wait_ge(ho_ready, 2 * l + p + 1)
                    nc.scalar.activation(br_hi[:, 4 + 2 * p:6 + 2 * p], K[:, 2 * p:2 * p + 2], ACT.Copy).then_inc(ho_hi, 1)
                for j in range(4):
                    act.wait_ge(merged_ready, 4 * l + j + 1)
                    nc.scalar.activation(x_hi[:, 2 * j:2 * j + 2], T0[:, 2 * j:2 * j + 2], ACT.Copy, scale=0.5).then_inc(merged_hi, 1)
                    ahead.to(c0 + 22 + j + 4)
                for j in range(4):
                    square(s + 1, 2 * j, width=2)
                    ahead.to(c0 + 26 + j + 4)

            def bias_rows():
                for h in range(8):
                    act.wait_ge(e["rel_done"], h + 1)
                    nc.scalar.activation(STAGE[:, h * 384:(h + 1) * 384], aux[:, h % 2, 0:384], ACT.Copy).then_inc(e["rel_copied"], 1)
                act.wait_ge(e["rel_copied"], 8)
                act.dma_start(skew.rearrange("h (p w) -> p h w", p=P), STAGE.rearrange("p (h w) -> p h w", h=8)).then_inc(e["skew_stored"], 16)

            def copy(c, to, scale=1.0):
                act.wait_ge(chunk_done, c + 1)
                nc.scalar.activation(flat(to), acc[:, c % RING, :], ACT.Copy, scale=scale).then_inc(acc_taken[c % RING], 1)
                ahead.to(c + 4)

            def mix2(s, l):
                c0 = base[s]
                for j in range(2):
                    copy(c0 + j, IQ[:, 2 * j:2 * j + 2])
                c = c0 + 2
                act.wait_ge(chunk_done, c + 1)
                ac(nc.scalar.activation(IK, acc[:, c % RING, 0:S], ACT.Copy))
                nc.scalar.activation(CKT, acc[:, c % RING, S:2 * S], ACT.Copy).then_inc(acc_taken[c % RING], 1)
                act.wait_ge(acc_taken[c % RING], turns.before[c] + 1)
                for tt in range(2):
                    nc.scalar.activation(JUNK[:, tt * P:(tt + 1) * P], CKT[:, tt * P:(tt + 1) * P], ACT.Square,
                                         accum_out=CKS[:, tt:tt + 1]).then_inc(e["ck_sq"], 1)
                ahead.to(c + 4)
                act.wait_ge(e["ck_var"], l + 1)
                nc.scalar.activation(CKS[:, 4:6], CKS[:, 2:4], ACT.Sqrt).then_inc(e["ck_sd"], 1)
                copy(c0 + 3, QA[:, 0:2], 0.125)
                for h in range(8):
                    act.wait_ge(e["dots_done"], 8 * l + h + 1)
                    if h >= 2:
                        act.wait_ge(e["score_ready"], 8 * l + h - 1)
                    nc.scalar.activation(R(h), aux[:, h % 2, 0:384], ACT.Relu).then_inc(e["dots_relu"], 1)
                copy(c0 + 4, QA[:, 2:4], 0.125)
                act.wait_ge(e["ck_turned"], l + 1)
                nc.scalar.activation(CKF, aux[:, 0, 0:S], ACT.Copy).then_inc(e["ckf_ready"], 1)

                def conv_gate(p):
                    c = c0 + 5 + 3 * p
                    if p == 1:
                        act.wait_ge(acc_taken[(c0 + 6) % RING], turns.before[c0 + 6] + 1)
                    copy(c, CC)

                conv_gate(0)
                for q in range(4):
                    act.wait_ge(e["lat_done"], 4 * l + q + 1)
                    h = 4 * (q // 2) + q % 2
                    nc.scalar.activation(QL[:, h:h + 3:2], aux[:, q % 2, :].rearrange("p (a b) -> p a b", a=2),
                                         ACT.Copy).then_inc(e["lat_ready"], 1)
                ahead.to(c0 + 6 + 4)
                ahead.to(c0 + 7 + 4)
                act.wait_ge(acc_taken[(c0 + 7) % RING], turns.before[c0 + 7] + 1)
                nc.scalar.activation(br_hi[:, 8:10], CY, ACT.Copy).then_inc(e["conv_hi"], 1)
                conv_gate(1)
                ahead.to(c0 + 10 + 4)
                act.wait_ge(acc_taken[(c0 + 10) % RING], turns.before[c0 + 10] + 1)
                nc.scalar.activation(br_hi[:, 10:12], CY, ACT.Copy).then_inc(e["conv_hi"], 1)
                copy(c0 + 11, QS[:, 0:2], 0.125)
                copy(c0 + 12, QS[:, 2:4], 0.125)
                copy(c0 + 13, KS[:, 0:2])
                copy(c0 + 14, KS[:, 2:4])
                for b in range(2):
                    act.wait_ge(e["max_ready"], 2 * l + b + 1)
                    for h in range(8):
                        lg = (flat(L0)[:, h * P:(h + 1) * P], L1[:, h])[b]
                        nc.scalar.activation(lg, lg, ACT.Exp, bias=MX[:, 8 * b + h:8 * b + h + 1],
                                             accum_out=SUM[:, 8 * b + h:8 * b + h + 1]).then_inc(e["probs_exp"], 1)
                    ahead.to(c0 + 15 + b + 4)
                act.wait_ge(chunk_done, c0 + 16 + 1)
                for tt in range(2):
                    cc_ = c0 + 15 + tt
                    nc.scalar.activation(flat(VS[:, 2 * tt:2 * tt + 2]), acc[:, cc_ % RING, :], ACT.Copy).then_inc(acc_taken[cc_ % RING], 1)
                ahead.to(c0 + 16 + 4)

                def gate(n):
                    c = c0 + 17 + 2 * n
                    act.wait_ge(chunk_done, c + 1)
                    if n == 0:
                        act.wait_ge(e["gate_bias"], l + 1)
                    if n >= 2:
                        act.wait_ge(acc_taken[(c - 3) % RING], turns.before[c - 3] + 1)
                    for tl in range(2):
                        i = ((2, 0, 1)[n // 4]) * 8 + 2 * (n % 4) + tl
                        ins = nc.scalar.activation(GT(n)[:, tl], acc[:, c % RING, tl * S:(tl + 1) * S], ACT.Tanh,
                                                   bias=BG[:, i:i + 1], scale=0.5)
                        if tl:
                            ins.then_inc(acc_taken[c % RING], 1)
                        else:
                            ac(ins)
                    ahead.to(c + 4)

                def branch(n):
                    ahead.to(c0 + 18 + 2 * n + 4)

                gate(0)
                for n in range(6):
                    act.wait_ge(e["turned"], 6 * l + n + 1)
                    to = PT0[:, 2 * n:2 * n + 2] if n < 2 else PT1[:, 2 * n - 4:2 * n - 2]
                    nc.scalar.activation(flat(to), aux[:, n % 2, :], ACT.Copy).then_inc(e["turned_copied"], 1)
                branch(0)
                for n in range(4):
                    act.wait_ge(e["ol_done"], 4 * l + n + 1)
                    g = n % 2
                    to = OL[:, 4 * g:4 * g + 4, (n // 2) * P:(n // 2 + 1) * P]
                    nc.scalar.activation(to, aux[:, g, :].rearrange("p (h t) -> p h t", h=4), ACT.Copy).then_inc(e["ol_ready"], 1)
                gate(1)
                for n in range(2):
                    act.wait_ge(e["ya_done"], 2 * l + n + 1)
                    nc.scalar.activation(br_hi[:, 2 * n:2 * n + 2].rearrange("p a b -> p (a b)"), aux[:, n, :], ACT.Copy).then_inc(e["ya_hi"], 1)
                branch(1)

                def soft(h):
                    act.wait_ge(e["z_done"], 8 * l + h + 1)
                    if h >= 2:
                        act.wait_ge(e["arg_done"], 8 * l + h - 1)
                    ac(nc.scalar.activation(SP(h), aux[:, h % 2, 0:384], ACT.Abs))
                    ac.settle()
                    ac(nc.scalar.activation(SP(h), SP(h), ACT.Exp, scale=-1.0))
                    ac.settle()
                    nc.scalar.activation(SP(h), SP(h), ACT.Ln, bias=1.0).then_inc(e["zl_ready"], 1)

                def weights(h):
                    act.wait_ge(e["arg_done"], 8 * l + h + 1)
                    if h >= 2:
                        act.wait_ge(e["yb_done"], 8 * l + h - 1)
                    nc.scalar.activation(AW(h), (stat, bc)[h % 2][:, 0:384], ACT.Exp).then_inc(e["a_exp"], 1)

                def heads_hi(h):
                    act.wait_ge(e["yb_done"], 8 * l + h + 1)
                    r = slice(64 * (h % 2), 64 * (h % 2) + 64)
                    nc.scalar.activation(br_hi[r, 4 + h // 2], (stat, bc)[h % 2][r, 0:S], ACT.Copy).then_inc(e["yb_hi"], 1)

                def step(q):
                    (branch if q % 2 else gate)(2 + q // 2)

                soft(0)
                for h in range(8):
                    step(h)
                    if h < 7:
                        soft(h + 1)
                    weights(h)
                    if h:
                        heads_hi(h - 1)
                step(8)
                heads_hi(7)
                for q in range(9, 12):
                    step(q)
                for n in range(8, 12):
                    gate(n)
                    c = c0 + 18 + 2 * n
                    act.wait_ge(acc_taken[c % RING], turns.before[c] + 1)
                    nc.scalar.activation(mg_hi[:, 2 * n - 16:2 * n - 14], MG[:, 2 * n - 16:2 * n - 14], ACT.Copy,
                                         scale=0.5).then_inc(e["mg_hi"], 1)
                    branch(n)
                choose_sqrt()
                act.wait_ge(chunk_done, c0 + 40 + 1)
                act.wait_ge(e["mem_loaded"], 32 * (l + 1))
                for j in range(4):
                    nc.scalar.activation(br_hi[:, 2 * j:2 * j + 2], MEM[j], ACT.Copy).then_inc(e["mem_hi"], 1)
                    square(s + 1, 2 * j, width=2)
                    ahead.to(c0 + 41 + j + 4)

            def cross(s, l):
                c0 = base[s]
                for j in range(2):
                    copy(c0 + j, XK[:, 2 * j:2 * j + 2])
                act.wait_ge(chunk_done, c0 + 4)
                for tt in range(2):
                    nc.scalar.activation(flat(XV[:, 2 * tt:2 * tt + 2]), acc[:, (c0 + 2 + tt) % RING, :], ACT.Copy)\
                        .then_inc(acc_taken[(c0 + 2 + tt) % RING], 1)
                ahead.to(c0 + 3 + 4)
                for j in range(2):
                    copy(c0 + 4 + j, XQ[:, 2 * j:2 * j + 2], float(P) ** -0.5)
                banks = [aux[:, 0, :], aux[:, 1, :], stat[:, :], bc[:, :]]
                for n in range(4):
                    act.wait_ge(e["xmax_ready"], 4 * l + n + 1)
                    for hh in range(2):
                        nc.scalar.activation(XL[:, 2 * n + hh], banks[n][:, hh * S:(hh + 1) * S], ACT.Exp,
                                             bias=MX[:, 2 * n + hh:2 * n + hh + 1],
                                             accum_out=SUM[:, 2 * n + hh:2 * n + hh + 1]).then_inc(e["x_exp"], 1)
                for n in range(4):
                    act.wait_ge(e["xt_done"], 4 * l + n + 1)
                    nc.scalar.activation(flat(XPT[:, 2 * n:2 * n + 2]), banks[n], ACT.Copy).then_inc(e["xt_copied"], 1)
                for p in range(2):
                    act.wait_ge(e["xo_done"], 2 * l + p + 1)
                    nc.scalar.activation(flat(br_hi[:, 8 + 2 * p:10 + 2 * p]), aux[:, p, :], ACT.Copy).then_inc(e["xo_hi"], 1)
                choose_sqrt()
                for j in range(4):
                    square(s + 1, 2 * j, width=2)
                    ahead.to(c0 + 6 + j + 4)

            for n in range(KD):
                square(0, n)
            act.wait_ge(consts_set, 3)
            choose_sqrt()
            act.wait_ge(consts_loaded, 16 * N_CONSTS)
            for N in range(n_norms):
                norm(N)
                if N == 0:
                    ahead.to(3)
                if N < n_subs:
                    if subs[N] == "ffn":
                        ffn(N, subs[:N].count("ffn"))
                    if subs[N] == "mix1":
                        mix1(N, subs[:N].count("mix1"))
                    if subs[N] == "mix2":
                        mix2(N, subs[:N].count("mix2"))
                    if subs[N] == "cross":
                        cross(N, subs[:N].count("cross"))

        @block.vector
        def _(dve):
            vc = Chain(dve, v_chain)
            ahead = Ahead(dve, split_lo)
            V_ = nc.vector

            def norm(N):
                dve.wait_ge(stat_done, N + 1)
                eps = EPS2 if centred(N) else EPS1
                if centred(N):
                    vc(V_.tensor_copy(small[:, 4:6], stat[:, 0:4:2]))
                    vc.settle()
                    vc(V_.tensor_tensor(small[:, 6:8], small[:, 4:6], small[:, 4:6], ALU.mult))
                    vc.settle()
                    V_.scalar_tensor_tensor(small[:, 0:2], stat[:, 1:4:2], eps, small[:, 6:8], ALU.add,
                                            ALU.subtract).then_inc(var_ready, 1)
                else:
                    V_.tensor_scalar(small[:, 0:2], stat[:, 1:4:2], eps, None, ALU.add).then_inc(var_ready, 1)
                dve.wait_ge(sd_ready, N + 1)
                vc(V_.reciprocal(small[:, 24:26], small[:, 2:4]))
                vc.settle()
                if centred(N):
                    vc(V_.scalar_tensor_tensor(small[:, 26:28], small[:, 4:6], -1.0, small[:, 24:26], ALU.mult, ALU.mult))
                    vc.settle()
                for q in range(4 if centred(N) else 2):
                    ins = V_.tensor_scalar(diag[:, q * P:(q + 1) * P], ident[:, :], small[:, 24 + q:25 + q], None, ALU.mult)
                    if q == (3 if centred(N) else 1):
                        ins.then_inc(diag_ready, 1)
                if N == 0:
                    ahead.to(0)
                dve.wait_ge(bc_done, N + 1)

                def tile(n):
                    if centred(N):
                        vc(V_.tensor_tensor(T[:, n], x[:, n], bc[:, 0:S], ALU.mult))
                        vc.settle()
                        V_.tensor_tensor(T[:, n], T[:, n], bc[:, S:2 * S], ALU.add).then_inc(t_ready, 1)
                    else:
                        V_.tensor_tensor(T[:, n], x[:, n], bc[:, 0:S], ALU.mult).then_inc(t_ready, 1)

                def lo(n):
                    if not parts(N):
                        return
                    dve.wait_ge(xh_ready, KD * N + n + 1)
                    if replaces(N):
                        V_.tensor_tensor(x_lo[:, n], x[:, n], x_hi[:, n].bitcast(F32), ALU.subtract).then_inc(x_parts, 1)
                    else:
                        V_.scalar_tensor_tensor(x_lo[:, n], T[:, n], norm_g[:, KD * N + n:KD * N + n + 1],
                                                x_hi[:, n].bitcast(F32), ALU.mult, ALU.subtract).then_inc(x_parts, 1)

                for n in range(KD):
                    tile(n)
                    if n:
                        lo(n - 1)
                lo(KD - 1)

            def ffn(s, f):
                c0 = base[s]

                def pair(p, turn=0):
                    g = c0 + 2 * p
                    dve.wait_ge(acc_taken[g % RING], turns.before[g] + 1 + turn)
                    dve.wait_ge(chunk_done, g + 2 + 4 * turn)
                    V_.tensor_tensor(flat(HID(p)), flat(SIL(p)), acc[:, (g + 1) % RING, :], ALU.mult)\
                        .then_inc(acc_taken[(g + 1) % RING], 1)
                    dve.wait_ge(hid_hi, 11 * f + p + 1 + 2 * turn)
                    at = bass.ds(2 * p + 4 * turn, 2)
                    V_.tensor_tensor(h_lo[:, at], HID(p), h_hi[:, at].bitcast(F32), ALU.subtract)\
                        .then_inc(hid_parts, 1)

                with dve.Fori(0, 4) as i:
                    for p in range(2):
                        c = c0 + 2 * p
                        split_lo(dve, c + 4, c % RING, WIDE, used=4 * i)
                        pair(p, i)
                        split_lo(dve, c + 5, (c + 1) % RING, WIDE, used=4 * i)
                ahead.next = c0 + 20
                for p in range(8, 11):
                    ahead.to(c0 + 2 * p + 4)
                    pair(p)
                    ahead.to(c0 + 2 * p + 5)
                c1 = c0 + UP_CHUNKS

                def sum_tile(n, turn=0, tile=0):
                    b = c1 + 2 * n + 1
                    dve.wait_ge(chunk_done, b + 1 + 4 * turn)
                    xt = x[:, bass.ds(n + tile, 1)]
                    if s >= 6:
                        if n == 0 or n == 6:
                            dve.wait_ge(x_scaled, s - 6 + 1)
                    out = xt.rearrange("p a b -> p (a b)")
                    V_.scalar_tensor_tensor(out, acc[:, b % RING, 0:S], 0.5, out, ALU.mult, ALU.add)\
                        .then_inc(acc_taken[b % RING], 1)

                with dve.Fori(0, 3) as i:
                    for n in range(2):
                        sum_tile(n, i, 2 * i)
                        for u in range(2):
                            c = c1 + 2 * n + u
                            split_lo(dve, c + 4, c % RING, DOWN, used=4 * i)
                ahead.next = c1 + 16
                for n in range(6, 8):
                    sum_tile(n)
                    ahead.to(c1 + 2 * n + 1 + 4)

            def mix1(s, l):
                c0 = base[s]
                dve.wait_ge(mixer_loaded, 16 * N_MIXER)
                hg = lambda h: cols1[:, l, 1, h:h + 1]
                if l:
                    lo0, lo1 = cols1[:, 0, 2, :], cols1[:, 1, 2, :]
                    L = lambda j: lbc[:, j, :]
                    vc(V_.tensor_tensor(L(0), lo0, lo1, ALU.max))
                    vc.settle()
                    vc(V_.tensor_tensor(L(2), lo0, L(0), ALU.subtract))
                    V_.tensor_tensor(L(3), lo1, L(0), ALU.subtract).then_inc(lb_ready, 1)
                    dve.wait_ge(lb_exp, 1)
                    vc(V_.tensor_tensor(L(4), L(2), L(3), ALU.add))
                    vc.settle()
                    vc(V_.reciprocal(L(4), L(4)))
                    vc.settle()
                    vc(V_.tensor_tensor(L(5), L(2), L(4), ALU.mult))
                    vc(V_.tensor_tensor(L(6), L(3), L(4), ALU.mult))
                    vc.settle()
                    vc(V_.tensor_tensor(L(6), L(5), L(6), ALU.add))
                    vc.settle()
                    vc(V_.tensor_tensor(L(6), L(6), L(5), ALU.subtract))
                    vc.settle()
                    vc(V_.tensor_scalar(L(7), L(6), -1.0, 1.0, ALU.mult, ALU.add))
                    vc.settle()
                    vc(V_.tensor_scalar(L(8), L(6), 2.0 ** -63, None, ALU.max))
                    V_.tensor_scalar(L(9), L(7), 2.0 ** -63, None, ALU.max).then_inc(lb_ready, 1)
                    dve.wait_ge(lb_logs, 1)
                    vc(V_.tensor_tensor(L(10), L(9), L(8), ALU.subtract))
                for p in range(2):
                    c = c0 + p
                    ps = acc[:, c % RING, :]
                    fa, fl, lf, k = (flat(v[:, 2 * p:2 * p + 2]) for v in (FA, FL, LF, K))
                    ahead.to(c + 4)
                    dve.wait_ge(chunk_done, c + 1)
                    dve.wait_ge(f_ln, 2 * l + p + 1)
                    vc(V_.scalar_tensor_tensor(lf, ps, 0.0, fl, ALU.min, ALU.subtract))
                    V_.scalar_tensor_tensor(fa, ps, 0.0, fl, ALU.max, ALU.add).then_inc(acc_taken[c % RING], 1)
                    ahead.to(c + 4)
                    vc.settle()
                    if l:
                        dve.wait_ge(k_exp, 2 * l + p + 1)
                        for h in (2 * p, 2 * p + 1):
                            vc(V_.tensor_scalar(K[:, h], K[:, h], lbc[:, 7, h:h + 1], None, ALU.mult))
                        vc(V_.tensor_scalar(FA[:, 2 * p], LF[:, 2 * p], lbc[:, 10, 2 * p:2 * p + 1], None, ALU.add))
                        vc.settle()
                        V_.tensor_scalar(FA[:, 2 * p + 1], LF[:, 2 * p + 1], lbc[:, 10, 2 * p + 1:2 * p + 2], None,
                                         ALU.add).then_inc(la_d, 1)
                        dve.wait_ge(la_d, p + 1)
                        for h in (2 * p, 2 * p + 1):
                            vc(V_.tensor_scalar(LF[:, h], FA[:, h], 0.0, lbc[:, 8, h:h + 1], ALU.max, ALU.add))
                        vc.settle()
                        dve.wait_ge(la_ln, p + 1)
                        vc(V_.tensor_tensor(lf, lf, fl, ALU.add))
                        vc.settle()
                    for h in (2 * p, 2 * p + 1):
                        for b in range(2):
                            part = LF[:, h, b * P:(b + 1) * P]
                            ins = V_.tensor_tensor_scan(part, ones[:, :], part, 0.0, ALU.mult, ALU.add)
                            if h == 2 * p + 1 and b:
                                ins.then_inc(forget_ready, 1)
                            else:
                                vc(ins)
                vc.settle()
                for p in range(2):
                    c = c0 + 2 + p
                    dve.wait_ge(qog_tanh, 4 * l + p + 1)
                    V_.scalar_tensor_tensor(flat(Q[:, 2 * p:2 * p + 2]), flat(QT[:, 2 * p:2 * p + 2]), 1.0,
                                            acc[:, c % RING, :], ALU.add, ALU.mult).then_inc(acc_taken[c % RING], 1)
                    ahead.to(c + 4)
                for j in range(4, 8):
                    ahead.to(c0 + j + 4)
                for p in range(2):
                    c = c0 + 8 + p
                    dve.wait_ge(qog_tanh, 4 * l + p + 3)
                    V_.scalar_tensor_tensor(flat(OG[:, 2 * p:2 * p + 2]), flat(QT[:, 4 + 2 * p:6 + 2 * p]), 1.0,
                                            acc[:, c % RING, :], ALU.add, ALU.mult).then_inc(acc_taken[c % RING], 1)
                    ahead.to(c + 4)
                dve.wait_ge(pooled_sum, l + 1)
                sums = [SUM0[:, 0], SUM1[:, 1], SUM0[:, 2], SUM1[:, 3]]
                first = FA[:, 0:1].rearrange("p a b -> p (a b)")[:, 0:64].rearrange("p (g c) -> p g c", g=4)
                for g in range(4):
                    vc(V_.tensor_tensor(first[:, g], sums[g][:, 0:16], counts[:, g], ALU.mult))
                vc.settle()
                vc(V_.tensor_tensor(first, first, U[:, :, 0:16], ALU.subtract))
                vc.settle()
                for g in range(4):
                    vc(V_.scalar_tensor_tensor(U[:, g], sums[g], 1.0 / WINDOWS[g], U[:, g], ALU.mult, ALU.subtract))
                vc.settle()
                V_.tensor_copy(U[:, :, 0:16], first).then_inc(pooled_ready, 1)
                for p in range(2):
                    dve.wait_ge(acc_taken[(c0 + 8 + p) % RING], turns.before[c0 + 8 + p] + 1)
                for h in range(4):
                    vc(V_.tensor_scalar(OG[:, h], OG[:, h], hg(h), 0.5, ALU.mult, ALU.mult))
                ahead.to(c0 + 10 + 4)
                for g in range(4):
                    dve.wait_ge(pool_hi, 4 * l + 2 * (g // 2) + 2)
                    V_.scalar_tensor_tensor(br_lo[:, g], aux[:, g // 2, (g % 2) * S:(g % 2 + 1) * S],
                                            cols1[:, l, 0, g:g + 1], br_hi[:, g].bitcast(F32), ALU.mult,
                                            ALU.subtract).then_inc(pool_parts, 1)

                def distance(n):
                    if n < 2 or n > 17:
                        return
                    li, hp = UNITS[n]
                    b = LF[:, 2 * hp:2 * hp + 2]
                    if n >= 4:
                        dve.wait_ge(lev_k, 16 * l + n - 3)
                        dve.wait_ge(lev_q, 16 * l + n - 3)
                    if li == 8:
                        vc(V_.tensor_tensor(EB(n)[:, :, 0:P], b[:, :, 0:P],
                                            b[:, :, P - 1:P].to_broadcast([P, 2, P]), ALU.subtract))
                        V_.tensor_copy(EB(n)[:, :, P:S], b[:, :, P:S]).then_inc(lev_d, 1)
                    else:
                        w = 2 * LEVELS[li]
                        bb = flat(b).rearrange("p (g w) -> p g w", w=w)
                        V_.tensor_tensor(flat(EB(n)).rearrange("p (g w) -> p g w", w=w), bb,
                                         bb[:, :, w // 2 - 1:w // 2].to_broadcast([P, 2 * S // w, w]),
                                         ALU.subtract).then_inc(lev_d, 1)

                def queries(n):
                    li, hp = UNITS[n]
                    if li == 7:
                        return
                    dve.wait_ge(lev_e, 16 * l + n - 1)
                    if n >= 4:
                        dve.wait_ge(lev_done, 18 * l + n - 1)
                    V_.tensor_tensor(flat(QB(n)), flat(Q[:, 2 * hp:2 * hp + 2]), flat(EB(n)), ALU.mult).then_inc(lev_q, 1)

                def keep(n):
                    if n < 0:
                        return
                    li, hp = UNITS[n]
                    dve.wait_ge(lev_done, 18 * l + n + 1)
                    if li == 8:
                        V_.tensor_copy(A2[:, hp], aux[:, n % 2, 0:S]).then_inc(lev_taken, 1)
                    else:
                        if n >= 2:
                            dve.wait_ge(lev_taken, 18 * l + n - 1)
                        V_.copy_predicated(A[:, 2 * hp:2 * hp + 2].rearrange("p h (b t) -> p (h b) t", b=2),
                                           levels[:, li:li + 1].bitcast(U32).to_broadcast([P, 4, P]),
                                           aux[:, n % 2, :].rearrange("p (a t) -> p a t", t=P)).then_inc(lev_taken, 1)

                dve.wait_ge(a_zeroed, l + 1)
                dve.wait_ge(forget_ready, 2 * l + 2)
                for j in range(8):
                    for n in (2 * j, 2 * j + 1):
                        distance(n + 1)
                        queries(n)
                        keep(n - 1)
                    ahead.to(c0 + 10 + j + 4)
                for n in (16, 17):
                    distance(n + 1)
                    queries(n)
                    keep(n - 1)
                keep(17)

                def pool_gate(j):
                    c = c0 + 18 + j
                    dve.wait_ge(chunk_done, c + 1)
                    V_.scalar_tensor_tensor(flat(T0[:, 2 * j:2 * j + 2]), flat(T0[:, 2 * j:2 * j + 2]), 1.0,
                                            acc[:, c % RING, :], ALU.add, ALU.mult).then_inc(acc_taken[c % RING], 1)
                    ahead.to(c + 4)

                pool_gate(0)
                for p in range(2):
                    dve.wait_ge(o_done, 2 * l + p + 1)
                    if p == 0:
                        vc.settle()
                    dve.wait_ge(o_sq, 2 * l + p + 1)
                    V_.tensor_tensor(flat(Q[:, 2 * p:2 * p + 2]), flat(OG[:, 2 * p:2 * p + 2]), aux[:, p, :],
                                     ALU.mult).then_inc(o_copied, 1)
                pool_gate(1)
                dve.wait_ge(o_stat, l + 1)
                V_.tensor_scalar(small[:, 8:16], stat[:, 0:8], EPS1, None, ALU.add).then_inc(o_var, 1)
                dve.wait_ge(o_sd, l + 1)
                vc(V_.reciprocal(small[:, 8:16], small[:, 16:24]))
                vc.settle()
                dve.wait_ge(o_copied, 2 * (l + 1))
                V_.tensor_tensor(flat(QT[:, 4:8]).rearrange("p (a b) -> p a b", a=8),
                                 ident[:, None, :].to_broadcast([P, 8, P]),
                                 small[:, 8:16, None].to_broadcast([P, 8, P]), ALU.mult).then_inc(o_diag, 1)
                pool_gate(2)
                pool_gate(3)
                for p in range(2):
                    dve.wait_ge(o_bc, 2 * l + p + 1)
                    V_.tensor_tensor(flat(K[:, 2 * p:2 * p + 2]), flat(Q[:, 2 * p:2 * p + 2]), aux[:, p, :],
                                     ALU.mult).then_inc(ho_ready, 1)
                for p in range(2):
                    dve.wait_ge(ho_hi, 2 * l + p + 1)
                    V_.tensor_tensor(br_lo[:, 4 + 2 * p:6 + 2 * p], K[:, 2 * p:2 * p + 2],
                                     br_hi[:, 4 + 2 * p:6 + 2 * p].bitcast(F32), ALU.subtract).then_inc(ho_parts, 1)
                for j in range(4):
                    c = c0 + 22 + j
                    t0, t1 = flat(T0[:, 2 * j:2 * j + 2]), flat(T1[:, 2 * j:2 * j + 2])
                    dve.wait_ge(chunk_done, c + 1)
                    dve.wait_ge(acc_taken[(c0 + 18 + j) % RING], turns.before[c0 + 18 + j] + 1)
                    V_.scalar_tensor_tensor(t1, t1, 1.0, acc[:, c % RING, :], ALU.add, ALU.mult).then_inc(acc_taken[c % RING], 1)
                    dve.wait_ge(acc_taken[c % RING], turns.before[c] + 1)
                    V_.tensor_tensor(t0, t0, t1, ALU.add).then_inc(merged_ready, 1)
                    dve.wait_ge(merged_hi, 4 * l + j + 1)
                    V_.scalar_tensor_tensor(flat(x_lo[:, 2 * j:2 * j + 2]), t0, 0.5, flat(x_hi[:, 2 * j:2 * j + 2]).bitcast(F32),
                                            ALU.mult, ALU.subtract).then_inc(merged_parts, 1)
                    ahead.to(c + 4)
                for j in range(4):
                    c = c0 + 26 + j
                    dve.wait_ge(chunk_done, c + 1)
                    xt = flat(x[:, 2 * j:2 * j + 2])
                    V_.tensor_tensor(xt, xt, acc[:, c % RING, :], ALU.add).then_inc(acc_taken[c % RING], 1)
                    ahead.to(c + 4)

            def add_out(s, c0, memory=None):
                for j in range(4):
                    c = c0 + j
                    dve.wait_ge(chunk_done, c + 1)
                    if j == 0:
                        dve.wait_ge(x_scaled, s - 5)
                    xt = flat(x[:, 2 * j:2 * j + 2])
                    V_.tensor_tensor(xt, xt, acc[:, c % RING, :], ALU.add).then_inc(acc_taken[c % RING], 1)
                    if memory is not None:
                        dve.wait_ge(e["mem_hi"], 4 * memory + j + 1)
                        V_.tensor_tensor(br_lo[:, 2 * j:2 * j + 2], MEM[j], br_hi[:, 2 * j:2 * j + 2].bitcast(F32),
                                         ALU.subtract).then_inc(e["mem_parts"], 1)
                    ahead.to(c + 4)

            def mix2(s, l):
                c0 = base[s]
                for j in range(3):
                    ahead.to(c0 + j + 4)
                dve.wait_ge(e["ck_sq"], 2 * (l + 1))
                V_.tensor_scalar(CKS[:, 2:4], CKS[:, 0:2], 1.0 / P, EPS2, ALU.mult, ALU.add).then_inc(e["ck_var"], 1)
                dve.wait_ge(e["iw_done"], l + 1)
                V_.tensor_scalar(IW, stat[:, 0:16], float(8 ** -0.5 * 64 ** -0.5), None, ALU.mult).then_inc(e["iw_ready"], 1)
                dve.wait_ge(e["small2_loaded"], 16 * (l + 1))
                V_.tensor_scalar(BG, BG, 0.5, None, ALU.mult).then_inc(e["gate_bias"], 1)
                dve.wait_ge(e["ck_sd"], l + 1)
                vc(V_.reciprocal(CKS[:, 6:8], CKS[:, 4:6]))
                vc.settle()
                vc(V_.scalar_tensor_tensor(CKT[:, 0:P], CKT[:, 0:P], CKS[:, 6:7], KVG, ALU.mult, ALU.mult))
                V_.scalar_tensor_tensor(CKT[:, P:S], CKT[:, P:S], CKS[:, 7:8], KVG, ALU.mult, ALU.mult).then_inc(e["ck_ready"], 1)
                ahead.to(c0 + 3 + 4)
                dve.wait_ge(e["iw_ready"], l + 1)
                for h in range(8):
                    dve.wait_ge(e["dots_relu"], 8 * l + h + 1)
                    parts_ = ((0, P, h), (P, 384, 8 + h))
                    if h:
                        dve.wait_ge(e["score_ready"], 8 * l + h)
                        vc.settle()
                    for q, (a, b, w) in enumerate(parts_):
                        if h == 0:
                            ins = V_.tensor_scalar(SC[:, a:b], R(h)[:, a:b], IW[:, w:w + 1], None, ALU.mult)
                        else:
                            ins = V_.scalar_tensor_tensor(SC[:, a:b], R(h)[:, a:b], IW[:, w:w + 1], SC[:, a:b], ALU.mult, ALU.add)
                        if q:
                            ins.then_inc(e["score_ready"], 1)
                        else:
                            vc(ins)
                ahead.to(c0 + 4 + 4)

                def conv(p):
                    c = c0 + 5 + 3 * p
                    ahead.to(c + 4)
                    dve.wait_ge(acc_taken[c % RING], turns.before[c] + 1)
                    dve.wait_ge(chunk_done, c + 2)
                    V_.tensor_tensor(flat(CZ), flat(CC), acc[:, (c + 1) % RING, :], ALU.mult).then_inc(acc_taken[(c + 1) % RING], 1)
                    ahead.to(c + 5)
                    dve.wait_ge(acc_taken[(c + 1) % RING], turns.before[c + 1] + 1)
                    if p:
                        dve.wait_ge(e["conv_parts"], 2 * l + p)
                    w = lambda tl, tap: CONV[:, 3 * (2 * p + tl) + tap:3 * (2 * p + tl) + tap + 1]
                    for tl in range(2):
                        vc(V_.tensor_scalar(CY[:, tl], CZ[:, tl], w(tl, 2), None, ALU.mult))
                    for back in (1, 2):
                        vc.settle()
                        for tl in range(2):
                            vc(V_.scalar_tensor_tensor(CY[:, tl, back:S], CZ[:, tl, 0:S - back], w(tl, 2 - back),
                                                       CY[:, tl, back:S], ALU.mult, ALU.add))
                    vc.settle()
                    dve.wait_ge(chunk_done, c + 3)
                    V_.tensor_tensor(flat(CY), flat(CY), acc[:, (c + 2) % RING, :], ALU.mult).then_inc(acc_taken[(c + 2) % RING], 1)
                    dve.wait_ge(acc_taken[(c + 2) % RING], turns.before[c + 2] + 1)
                    dve.wait_ge(e["conv_hi"], 2 * l + p + 1)
                    V_.tensor_tensor(br_lo[:, 8 + 2 * p:10 + 2 * p], CY, br_hi[:, 8 + 2 * p:10 + 2 * p].bitcast(F32),
                                     ALU.subtract).then_inc(e["conv_parts"], 1)
                    ahead.to(c + 6)

                def top(rounds):
                    for _ in range(rounds):
                        for a, b in ((0, P), (P, 384)):
                            m = M8 if a == 0 else sm[:, 80:88]
                            vc(V_.max(m, SC[:, a:b]))
                            vc.settle()
                            vc(V_.match_replace(SC[:, a:b], m, SC[:, a:b], TAKEN))
                        vc.settle()

                conv(0)
                dve.wait_ge(e["score_masked"], l + 1)
                top(3)
                conv(1)
                top(3)
                ahead.to(c0 + 11 + 4)
                top(2)
                ahead.to(c0 + 12 + 4)
                V_.tensor_scalar(PEN, SC, TAKEN, -1e30, ALU.not_equal, ALU.mult).then_inc(e["pen_ready"], 1)
                ahead.to(c0 + 13 + 4)
                ahead.to(c0 + 14 + 4)
                dve.wait_ge(e["pen_masked"], l + 1)
                dve.wait_ge(e["bias_loaded"], 16)
                for n in range(6):
                    dve.wait_ge(e["log_done"], 6 * l + n + 1)
                    if n < 4:
                        V_.tensor_tensor(L1[:, 2 * n:2 * n + 2], aux[:, n % 2, :].rearrange("p (a b) -> p a b", a=2),
                                         BIAS[:, 2 * n:2 * n + 2], ALU.add).then_inc(e["log_taken"], 1)
                    else:
                        q = n - 4
                        V_.tensor_tensor(flat(L0)[:, q * 512:(q + 1) * 512].rearrange("p (h t) -> p h t", h=4),
                                         aux[:, n % 2, :].rearrange("p (h t) -> p h t", h=4),
                                         BIAS[:, 4 * q:4 * q + 4, P:S], ALU.add).then_inc(e["log_taken"], 1)
                dve.wait_ge(e["log_taken"], 6 * (l + 1))
                l0 = flat(L0).rearrange("p (h t) -> p h t", h=8)
                for b, (lg, pen) in enumerate(((l0, PEN[:, None, 0:P]), (L1, PEN[:, None, P:384]))):
                    vc(V_.tensor_tensor(lg, lg, pen.to_broadcast([P, 8, lg.shape[2]]), ALU.add))
                    vc.settle()
                    vc(V_.tensor_reduce(MX[:, 8 * b:8 * b + 8], lg, AXX, ALU.max))
                    vc.settle()
                    V_.tensor_scalar(MX[:, 8 * b:8 * b + 8], MX[:, 8 * b:8 * b + 8], -1.0, None, ALU.mult).then_inc(e["max_ready"], 1)
                for b, lg in enumerate((l0, L1)):
                    dve.wait_ge(e["probs_exp"], 16 * l + 8 * (b + 1))
                    vc(V_.reciprocal(RIN[:, 8 * b:8 * b + 8], SUM[:, 8 * b:8 * b + 8]))
                    vc.settle()
                    V_.tensor_tensor(lg, lg, RIN[:, 8 * b:8 * b + 8, None].to_broadcast([P, 8, lg.shape[2]]),
                                     ALU.mult).then_inc(e["probs_ready"], 1)
                    ahead.to(c0 + 15 + b + 4)

                def gate(n):
                    ahead.to(c0 + 17 + 2 * n + 4)

                def branch(n):
                    c = c0 + 18 + 2 * n
                    dve.wait_ge(chunk_done, c + 1)
                    dve.wait_ge(acc_taken[(c - 1) % RING], turns.before[c - 1] + 1)
                    g, m = flat(GT(n)), flat(MG[:, 2 * (n % 4):2 * (n % 4) + 2])
                    if n < 4:
                        V_.scalar_tensor_tensor(m, g, 1.0, acc[:, c % RING, :], ALU.add, ALU.mult).then_inc(acc_taken[c % RING], 1)
                    else:
                        vc(V_.scalar_tensor_tensor(g, g, 1.0, acc[:, c % RING, :], ALU.add, ALU.mult))
                        vc.settle()
                        if n < 8:
                            p_ = c0 + 18 + 2 * (n - 4)
                            dve.wait_ge(acc_taken[p_ % RING], turns.before[p_] + 1)
                        V_.tensor_tensor(m, m, g, ALU.add).then_inc(acc_taken[c % RING], 1)
                    if n >= 8:
                        dve.wait_ge(acc_taken[c % RING], turns.before[c] + 1)
                        dve.wait_ge(e["mg_hi"], 4 * l + n - 7)
                        V_.scalar_tensor_tensor(flat(mg_lo[:, 2 * n - 16:2 * n - 14]), m, 0.5,
                                                flat(mg_hi[:, 2 * n - 16:2 * n - 14]).bitcast(F32), ALU.mult,
                                                ALU.subtract).then_inc(e["mg_parts"], 1)
                    ahead.to(c + 4)

                gate(0)
                branch(0)
                gate(1)
                for n in range(2):
                    dve.wait_ge(e["ya_hi"], 2 * l + n + 1)
                    V_.tensor_tensor(flat(br_lo[:, 2 * n:2 * n + 2]), aux[:, n, :], flat(br_hi[:, 2 * n:2 * n + 2]).bitcast(F32),
                                     ALU.subtract).then_inc(e["ya_parts"], 1)
                branch(1)

                def soft(h):
                    dve.wait_ge(e["zl_ready"], 8 * l + h + 1)
                    V_.scalar_tensor_tensor(SP(h), aux[:, h % 2, 0:384], 0.0, SP(h), ALU.max, ALU.add).then_inc(e["sp_ready"], 1)

                def heads_lo(h):
                    dve.wait_ge(e["yb_hi"], 8 * l + h + 1)
                    r = slice(64 * (h % 2), 64 * (h % 2) + 64)
                    V_.tensor_tensor(br_lo[r, 4 + h // 2], (stat, bc)[h % 2][r, 0:S], br_hi[r, 4 + h // 2].bitcast(F32),
                                     ALU.subtract).then_inc(e["yb_parts"], 1)

                def step(q):
                    (branch if q % 2 else gate)(2 + q // 2)

                soft(0)
                for h in range(8):
                    step(h)
                    if h < 7:
                        soft(h + 1)
                    if h:
                        heads_lo(h - 1)
                step(8)
                heads_lo(7)
                for q in range(9, 12):
                    step(q)
                for n in range(8, 12):
                    gate(n)
                    branch(n)
                add_out(s, c0 + 41, l)

            def cross(s, l):
                c0 = base[s]
                for j in range(6):
                    ahead.to(c0 + j + 4)
                banks = [aux[:, 0, :], aux[:, 1, :], stat[:, :], bc[:, :]]
                for n in range(4):
                    dve.wait_ge(e["xl_done"], 4 * l + n + 1)
                    vc(V_.tensor_reduce(MX[:, 2 * n:2 * n + 2], banks[n][:, :].rearrange("p (h t) -> p h t", h=2), AXX, ALU.max))
                    vc.settle()
                    V_.tensor_scalar(MX[:, 2 * n:2 * n + 2], MX[:, 2 * n:2 * n + 2], -1.0, None, ALU.mult).then_inc(e["xmax_ready"], 1)
                for n in range(4):
                    dve.wait_ge(e["x_exp"], 8 * l + 2 * n + 2)
                    vc(V_.reciprocal(RIN[:, 2 * n:2 * n + 2], SUM[:, 2 * n:2 * n + 2]))
                    vc.settle()
                    V_.tensor_tensor(XL[:, 2 * n:2 * n + 2], XL[:, 2 * n:2 * n + 2],
                                     RIN[:, 2 * n:2 * n + 2, None].to_broadcast([P, 2, S]), ALU.mult).then_inc(e["xp_ready"], 1)
                for p in range(2):
                    dve.wait_ge(e["xo_hi"], 2 * l + p + 1)
                    V_.tensor_tensor(flat(br_lo[:, 8 + 2 * p:10 + 2 * p]), aux[:, p, :],
                                     flat(br_hi[:, 8 + 2 * p:10 + 2 * p]).bitcast(F32), ALU.subtract).then_inc(e["xo_parts"], 1)
                add_out(s, c0 + 6)

            V_.memset(ones[:, :], 1.0).then_inc(consts_set, 1)
            V_.memset(mean_col[:, :], 1.0 / D).then_inc(consts_set, 1)
            V_.memset(mean_head[:, :], 1.0 / P).then_inc(consts_set, 1)
            dve.wait_ge(consts_set, 3)
            dve.wait_ge(consts_loaded, 16 * N_CONSTS)
            for N in range(n_norms):
                norm(N)
                if N == 0:
                    ahead.to(3)
                if N < n_subs:
                    if subs[N] == "ffn":
                        ffn(N, subs[:N].count("ffn"))
                    if subs[N] == "mix1":
                        mix1(N, subs[:N].count("mix1"))
                    if subs[N] == "mix2":
                        mix2(N, subs[:N].count("mix2"))
                    if subs[N] == "cross":
                        cross(N, subs[:N].count("cross"))

        @block.gpsimd
        def _(pool):
            gc = Chain(pool, g_chain)
            G_ = nc.gpsimd

            def mix1(s, l):
                c0 = base[s]
                pool.wait_ge(x_parts, KD * (s + 1))
                G_.memset(A[:, :, :], 0.0).then_inc(a_zeroed, 1)
                pool.dma_start(pool_w[:, :], t["pool_w"][l]).then_inc(pool_w_loaded, 16)
                for p in range(2):
                    pool.wait_ge(acc_taken[(c0 + 6 + p) % RING], turns.before[c0 + 6 + p] + 1)
                src = U
                for step, dst in enumerate((SUM0, SUM1, SUM0, SUM1)):
                    w = 1 << step
                    gc(G_.tensor_tensor(dst[:, step:4, w:S], src[:, step:4, w:S], src[:, step:4, 0:S - w], ALU.add))
                    gc(G_.tensor_copy(dst[:, step:4, 0:w], src[:, step:4, 0:w]))
                    gc.settle()
                    src = dst
                pool.wait_ge(pool_w_loaded, 16 * (l + 1))
                G_.tensor_copy(gdummy[:, :], gdummy[:, :]).then_inc(pooled_sum, 1)
                for n in range(2, 18):
                    li, hp = UNITS[n]
                    pool.wait_ge(lev_e, 16 * l + n - 1)
                    if n >= 4:
                        pool.wait_ge(lev_done, 18 * l + n - 1)
                    G_.tensor_tensor(flat(KB(n)), flat(K[:, 2 * hp:2 * hp + 2]), flat(EB(n)), ALU.mult).then_inc(lev_k, 1)

            gc(G_.memset(gdummy[:, :], 0.0))
            gc.settle()
            def load_small(l, s):
                pool.wait_ge(x_parts, KD * (s + 1))
                pool.dma_start(small2[:, :], t["small2"][l]).then_inc(e["small2_loaded"], 16)

            def scale_x(s):
                pool.wait_ge(x_parts, KD * (s + 1))
                if subs[s] == "mix2":
                    pool.wait_ge(e["iw_done"], subs[:s].count("mix2") + 1)
                G_.tensor_scalar(x[:, :, :], x[:, :, :], ALPHA, 0.0, ALU.mult, ALU.add).then_inc(x_scaled, 1)

            def mix2(s, l):
                scale_x(s)
                pool.wait_ge(e["score_ready"], 8 * (l + 1))
                gc(G_.affine_select(out=SC[:, 0:P], in_=SC[:, 0:P], pattern=[[-1, P]], compare_op=ALU.is_ge,
                                    fill=HIDDEN, base=0, channel_multiplier=1))
                G_.affine_select(out=SC[:, P:384], in_=SC[:, P:384], pattern=[[-1, S]], compare_op=ALU.is_ge,
                                 fill=HIDDEN, base=P, channel_multiplier=1).then_inc(e["score_masked"], 1)
                pool.wait_ge(e["pen_ready"], l + 1)
                gc(G_.affine_select(out=PEN[:, 0:P], in_=PEN[:, 0:P], pattern=[[-1, P]], compare_op=ALU.is_ge,
                                    fill=-1e30, base=0, channel_multiplier=1))
                G_.affine_select(out=PEN[:, P:384], in_=PEN[:, P:384], pattern=[[-1, S]], compare_op=ALU.is_ge,
                                 fill=-1e30, base=P, channel_multiplier=1).then_inc(e["pen_masked"], 1)

                def strict(v, done):
                    for q, a in enumerate((0, S)):
                        ins = G_.affine_select(out=v[:, a:a + P], in_=v[:, a:a + P], pattern=[[1, P]],
                                               compare_op=ALU.is_gt, fill=0.0, base=0, channel_multiplier=-1)
                        if q:
                            ins.then_inc(done, 1)
                        else:
                            gc(ins)

                for h in range(8):
                    if h == 0:
                        pool.wait_ge(e["sp_ready"], 8 * l + 1)
                        strict(SP(0), e["sp_masked"])
                    if h < 7:
                        pool.wait_ge(e["sp_ready"], 8 * l + h + 2)
                        strict(SP(h + 1), e["sp_masked"])
                    pool.wait_ge(e["a_exp"], 8 * l + h + 1)
                    strict(AW(h), e["a_masked"])
                pool.wait_ge(e["yb_parts"], 8 * (l + 1))
                for half_, to in enumerate((tmp[:, 20:24], gates[:, 16:20])):
                    src = t["mem"][:, half_ * 4 * S:(half_ + 1) * 4 * S].rearrange("p (a b) -> p a b", a=4)
                    pool.dma_start(to, src).then_inc(e["mem_loaded"], 16)

            def cross(s, l):
                scale_x(s)
                if l == 0:
                    load_small(1, s)

            for N in range(n_norms - 1):
                if N == 6:
                    pool.wait_ge(x_parts, KD * 6 + 1)
                    pool.dma_start(HOT, t["onehot"]).then_inc(e["rel_loaded"], 16)
                    pool.dma_start(REL, t["rel"]).then_inc(e["rel_loaded"], 16)
                    load_small(0, 6)
                if subs[N] == "mix1":
                    mix1(N, subs[:N].count("mix1"))
                if subs[N] == "mix2":
                    mix2(N, subs[:N].count("mix2"))
                if subs[N] == "cross":
                    cross(N, subs[:N].count("cross"))
                if subs[N] == "ffn" and N >= 6:
                    scale_x(N)


UNITS = [(7, 0), (7, 1)] + [(li, hp) for li in (0, 1, 2, 3, 4, 5, 6, 8) for hp in range(2)]
N_CONSTS = 2
N_MIXER = 4
HIDDEN, TAKEN = -3.0e38, -3.3e38


def host(i):
    i = {k: np.asarray(v) for k, v in i.items()}
    packed = pack(i)
    a = {f"w{k}": v for k, v in packed.items()}
    a["x"] = np.ascontiguousarray(i["x"][0].T.reshape(KD, P, S).transpose(1, 0, 2)).reshape(P, -1)
    gains = []
    for l in range(LAYERS):
        gains += [i["ffn1_norm"][l], i["mix_norm"][l], i["ffn2_norm"][l]]
    gains.append(i["final_norm"])
    for l in range(LAYERS):
        gains += [i["ln_g_2"][l, n] for n in range(4)]
    a["norm_g"] = columns(np.stack(gains))
    bias = [np.zeros(D, np.float32)] * 7 + [i["ln_b_2"][l, n] for l in range(LAYERS) for n in range(4)]
    a["norm_b"] = columns(np.stack(bias))
    a["cols1"] = columns(np.stack([i["pool_scale"], i["hgrn_norm"], i["lb_logits"]], 1))
    a["pool_w"] = np.ascontiguousarray(i["pool_w"].transpose(0, 2, 1, 3)).reshape(LAYERS, P, 4 * P)
    a.update(constants())
    a["mem"] = np.ascontiguousarray(i["mem_2"][0].T.reshape(KD, P, S).transpose(1, 0, 2)).reshape(P, -1)
    a["small2"] = small_weights(i)
    a["onehot"] = bucket_table()
    a["rel"] = np.ascontiguousarray(np.broadcast_to(i["rel_bias_2"][:, :, None], (32, 8, P))).reshape(32, -1)
    return a


def build(nc, shapes):
    t = {k: nc.dram_tensor("in_" + k, v, F32, kind="ExternalInput").ap() for k, v in shapes.items()}
    t["out"] = nc.dram_tensor("out", (P, KD * S), F32, kind="ExternalOutput").ap()
    program(nc, t)


def kernel(**inputs):
    import concourse.bacc as bacc
    from concourse.bass_utils import run_bass_kernel_spmd
    arrays = host(inputs)
    nc = bacc.Bacc("TRN2", target_bir_lowering=False, num_devices=1, dynamic_dma_scratch_size=1024)
    build(nc, {k: v.shape for k, v in arrays.items()})
    r = run_bass_kernel_spmd(nc, [{"in_" + k: v for k, v in arrays.items()}], core_ids=[0])
    out = np.asarray(r.results[0]["out"]).reshape(P, KD, S)
    return np.ascontiguousarray(out.transpose(2, 1, 0)).reshape(1, S, D)
```
